# Optimizing a Trainium2 kernel written in Bass

```python
import math
import jax, jax.numpy as jnp
from jax import lax
import numpy as np

D_MODEL = 1024
BATCH = 1
SEQ = 512
DEPTH = 2

GRID_W = 64
CTX_LEN = 256
D_MIX = D_MODEL
BRANCH_W = D_MIX // 2
A_HEADS = 8
A_QK = BRANCH_W // (2 * A_HEADS)
A_V = 2 * A_QK
CONV_W = 3
C_HEADS = 8
C_HEAD_DIM = BRANCH_W // C_HEADS
NA_KH = 8
NA_KW = 16
D_GROUPS = 8
D_GROUP_W = BRANCH_W // D_GROUPS
Q_BLOCK = 128
ROPE_BASE = 10000.0
EPS = 1e-6
N_EVEN = (DEPTH + 1) // 2
N_ODD = DEPTH // 2
EVEN_IN = 8 * BRANCH_W
ODD_IN = 6 * BRANCH_W


def rms_norm(x, g):
    xf = x.astype(jnp.float32)
    y = xf * lax.rsqrt(jnp.mean(xf * xf, axis=-1, keepdims=True) + EPS)
    return (y * g.astype(jnp.float32)).astype(x.dtype)

def lambda_init(layer):
    return 0.8 - 0.6 * math.exp(-0.3 * layer)

def axial_rope(x, row, col):
    half = x.shape[-1] // 2
    nf = half // 2
    inv_freq = ROPE_BASE ** (-jnp.arange(nf, dtype=jnp.float32) / nf)

    def rotate(u, pos):
        ang = pos.astype(jnp.float32)[:, None] * inv_freq
        cos = jnp.cos(ang)[None, :, None, None, :]
        sin = jnp.sin(ang)[None, :, None, None, :]
        u1, u2 = u[..., :nf], u[..., nf:]
        return jnp.concatenate([u1 * cos - u2 * sin, u2 * cos + u1 * sin], axis=-1)

    xf = x.astype(jnp.float32)
    y = jnp.concatenate([rotate(xf[..., :half], row), rotate(xf[..., half:], col)], axis=-1)
    return y.astype(x.dtype)

def diff_attend(q, k, v, lam):
    s = jnp.einsum('bqhmd,bkhmd->bhmqk', q, k).astype(jnp.float32) * (A_QK ** -0.5)
    p = jax.nn.softmax(s, axis=-1)
    a = p[:, :, 0] - lam * p[:, :, 1]
    return jnp.einsum('bhqk,bkhd->bqhd', a, v.astype(jnp.float32))

def diff_attention_post(o, subln, lam_init):
    B, N = o.shape[:2]
    return (rms_norm(o, subln) * (1.0 - lam_init)).reshape(B, N, BRANCH_W)

def short_conv(b, c, u, w):
    z = c * u
    y = lax.conv_general_dilated(z, w.reshape(CONV_W, 1, BRANCH_W).astype(z.dtype),
                                 window_strides=(1,), padding='SAME',
                                 dimension_numbers=('NWC', 'WIO', 'NWC'),
                                 feature_group_count=BRANCH_W)
    return b * y

def fourier_mix(u):
    B, N, _ = u.shape
    ug = u.astype(jnp.float32).reshape(B, N, D_GROUPS, D_GROUP_W)
    y = jnp.fft.fft2(ug, axes=(1, 3), norm='ortho').real
    return y.reshape(B, N, BRANCH_W).astype(u.dtype)

def dense_attend(q, k, v):
    s = jnp.einsum('bqhd,bkhd->bhqk', q, k).astype(jnp.float32) * (C_HEAD_DIM ** -0.5)
    p = jax.nn.softmax(s, axis=-1)
    return jnp.einsum('bhqk,bkhd->bqhd', p, v.astype(jnp.float32))

def neighbourhood_attention(q, k, v, k_c, v_c, rpb):
    B, S, H, d = q.shape
    rows = S // GRID_W
    kh = min(NA_KH, rows)
    kw = NA_KW
    r = jnp.arange(rows)
    cq = jnp.arange(GRID_W)
    rs = jnp.clip(r - kh // 2, 0, rows - kh)
    cs = jnp.clip(cq - kw // 2, 0, GRID_W - kw)
    col_idx = cs[:, None] + jnp.arange(kw)[None, :]
    row_off = rs[:, None] + jnp.arange(kh)[None, :] - r[:, None] + (NA_KH - 1)
    col_off = col_idx - cq[:, None] + (NA_KW - 1)
    scale = d ** -0.5
    qg = jnp.moveaxis(q.reshape(B, rows, GRID_W, H, d), 1, 0)
    kg = k.reshape(B, rows, GRID_W, H, d)
    vg = v.reshape(B, rows, GRID_W, H, d)
    s_c_all = None

    def one_row(args):
        q_r, r0, roff = args
        kb = lax.dynamic_slice_in_dim(kg, r0, kh, axis=1)
        vb = lax.dynamic_slice_in_dim(vg, r0, kh, axis=1)
        kwin = kb[:, :, col_idx]
        vwin = vb[:, :, col_idx]
        bias = rpb[:, roff][:, :, col_off]
        s_w = jnp.einsum('bqhd,biqjhd->bhqij', q_r, kwin).astype(jnp.float32) * scale
        s_w = s_w + jnp.transpose(bias, (0, 2, 1, 3))[None].astype(jnp.float32)
        s_w = s_w.reshape(B, H, GRID_W, kh * kw)
        s_c = jnp.einsum('bqhd,bkhd->bhqk', q_r, k_c).astype(jnp.float32) * scale
        p = jax.nn.softmax(jnp.concatenate([s_w, s_c], axis=-1), axis=-1)
        p_w = p[..., :kh * kw].reshape(B, H, GRID_W, kh, kw)
        p_c = p[..., kh * kw:]
        return (jnp.einsum('bhqij,biqjhd->bqhd', p_w, vwin.astype(jnp.float32))
                + jnp.einsum('bhqk,bkhd->bqhd', p_c, v_c.astype(jnp.float32)))

    o = lax.map(one_row, (qg, rs, row_off))
    return jnp.moveaxis(o, 0, 1).reshape(B, S, H * d)

def even_mixer(px, pc, lam_p, subln, conv_w, lam_init, row, col, need_ctx):
    B, S, _ = px.shape
    L = pc.shape[1]
    qa, ka, va, ga, bb, cb, ub, gb = jnp.split(px, 8, axis=-1)
    qa = axial_rope(qa.reshape(B, S, A_HEADS, 2, A_QK), row, col)
    ka = axial_rope(ka.reshape(B, S, A_HEADS, 2, A_QK), row, col)
    va = va.reshape(B, S, A_HEADS, A_V)
    if need_ctx:
        qc, kc, vc, gc, bbc, cbc, ubc, gbc = jnp.split(pc, 8, axis=-1)
    else:
        kc, vc = jnp.split(pc, 2, axis=-1)
    kc = kc.reshape(B, L, A_HEADS, 2, A_QK)
    vc = vc.reshape(B, L, A_HEADS, A_V)
    lp = lam_p.astype(jnp.float32)
    lam = jnp.exp(jnp.sum(lp[0] * lp[1])) - jnp.exp(jnp.sum(lp[2] * lp[3])) + lam_init
    k_all = jnp.concatenate([kc, ka], axis=1)
    v_all = jnp.concatenate([vc, va], axis=1)
    nb = S // Q_BLOCK
    q_blocks = jnp.moveaxis(qa.reshape(B, nb, Q_BLOCK, A_HEADS, 2, A_QK), 1, 0)
    o = lax.map(lambda qb: diff_attend(qb, k_all, v_all, lam), q_blocks)
    o = jnp.moveaxis(o, 0, 1).reshape(B, S, A_HEADS, A_V)
    out_a = diff_attention_post(o, subln, lam_init).astype(px.dtype) * jax.nn.silu(ga)
    out_b = short_conv(bb, cb, ub, conv_w) * jax.nn.silu(gb)
    out_x = jnp.concatenate([out_a, out_b], axis=-1)
    if not need_ctx:
        return out_x, None
    oc = diff_attend(qc.reshape(B, L, A_HEADS, 2, A_QK), kc, vc, lam)
    out_ac = diff_attention_post(oc, subln, lam_init).astype(pc.dtype) * jax.nn.silu(gc)
    out_bc = short_conv(bbc, cbc, ubc, conv_w) * jax.nn.silu(gbc)
    return out_x, jnp.concatenate([out_ac, out_bc], axis=-1)

def odd_mixer(px, pc, rpb, need_ctx):
    B, S, _ = px.shape
    L = pc.shape[1]

    def heads(u):
        return u.reshape(u.shape[0], u.shape[1], C_HEADS, C_HEAD_DIM)

    qn, kn, vn, gn, ud, gd = jnp.split(px, 6, axis=-1)
    if need_ctx:
        qc, kc, vc, gc, udc, gdc = jnp.split(pc, 6, axis=-1)
    else:
        kc, vc = jnp.split(pc, 2, axis=-1)
    kc, vc = heads(kc), heads(vc)
    o_n = neighbourhood_attention(heads(qn), heads(kn), heads(vn), kc, vc, rpb)
    out_x = jnp.concatenate([o_n.astype(px.dtype) * jax.nn.silu(gn),
                             fourier_mix(ud) * jax.nn.silu(gd)], axis=-1)
    if not need_ctx:
        return out_x, None
    o_nc = dense_attend(heads(qc), kc, vc).reshape(B, L, BRANCH_W)
    out_c = jnp.concatenate([o_nc.astype(pc.dtype) * jax.nn.silu(gc),
                             fourier_mix(udc) * jax.nn.silu(gdc)], axis=-1)
    return out_x, out_c

def first_inputs(seed: int = 0) -> dict:
    key = jax.random.key(seed)
    ks = jax.random.split(key, 15)
    f = jnp.float32
    nrm = jax.random.normal
    return {
        'x': nrm(ks[0], (BATCH, SEQ, D_MODEL), f),
        'c': nrm(ks[1], (BATCH, D_MODEL), f),
        'ctx': nrm(ks[2], (BATCH, CTX_LEN, D_MODEL), f),
        'c_ctx': nrm(ks[3], (D_MODEL,), f),
        'w_mod': nrm(ks[4], (DEPTH, D_MODEL, 3 * D_MODEL), f) * D_MODEL ** -0.5,
        'b_mod': 0.02 * nrm(ks[5], (DEPTH, 3 * D_MODEL), f),
        'norm_pre': 1.0 + 0.1 * nrm(ks[6], (DEPTH, D_MODEL), f),
        'norm_post': 1.0 + 0.1 * nrm(ks[7], (DEPTH, D_MODEL), f),
        'w_in_even': nrm(ks[8], (N_EVEN, D_MODEL, EVEN_IN), f) * D_MODEL ** -0.5,
        'lam_a': 0.1 * nrm(ks[9], (N_EVEN, 4, A_QK), f),
        'subln_a': 1.0 + 0.1 * nrm(ks[10], (N_EVEN, A_V), f),
        'conv_b': nrm(ks[11], (N_EVEN, CONV_W, BRANCH_W), f) * CONV_W ** -0.5,
        'w_in_odd': nrm(ks[12], (N_ODD, D_MODEL, ODD_IN), f) * D_MODEL ** -0.5,
        'rpb_c': 0.1 * nrm(ks[13], (N_ODD, C_HEADS, 2 * NA_KH - 1, 2 * NA_KW - 1), f),
        'w_out': nrm(ks[14], (DEPTH, D_MIX, D_MODEL), f) * D_MIX ** -0.5,
    }

def first_block(x, c, ctx, c_ctx, w_mod, b_mod, norm_pre, norm_post, w_in_even, lam_a,
              subln_a, conv_b, w_in_odd, rpb_c, w_out):
    S = x.shape[1]
    t = jnp.arange(S)
    row = t // GRID_W
    col = t % GRID_W
    silu_c = jax.nn.silu(c)
    silu_cc = jax.nn.silu(c_ctx)
    for l in range(DEPTH):
        need_ctx = l < DEPTH - 1
        j = l // 2
        mod_x = (silu_c @ w_mod[l] + b_mod[l])[:, None, :]
        mod_c = (silu_cc @ w_mod[l] + b_mod[l])[None, None, :]
        sh_x, sc_x, g_x = jnp.split(mod_x, 3, axis=-1)
        sh_c, sc_c, g_c = jnp.split(mod_c, 3, axis=-1)
        hx = rms_norm(x, norm_pre[l]) * (1.0 + sc_x) + sh_x
        hc = rms_norm(ctx, norm_pre[l]) * (1.0 + sc_c) + sh_c
        w_in = w_in_even[j] if l % 2 == 0 else w_in_odd[j]
        px = hx @ w_in
        pc = hc @ (w_in if need_ctx else w_in[:, BRANCH_W:3 * BRANCH_W])
        if l % 2 == 0:
            mx, mc = even_mixer(px, pc, lam_a[j], subln_a[j], conv_b[j], lambda_init(l),
                                row, col, need_ctx)
        else:
            mx, mc = odd_mixer(px, pc, rpb_c[j], need_ctx)
        x = x + g_x * rms_norm(mx @ w_out[l], norm_post[l])
        if need_ctx:
            ctx = ctx + g_c * rms_norm(mc @ w_out[l], norm_post[l])
    return x


N_MIXERS = 2
N_ATTN_LAYERS = (DEPTH + 1) // 2
N_SGU_LAYERS = DEPTH // 2

N_HEADS = 16
N_KV_HEADS = 4
HEAD_DIM = 64
Q_PER_KV = N_HEADS // N_KV_HEADS
WINDOW = 128
BLOCK = 128
Q_DIM = N_HEADS * HEAD_DIM
KV_DIM = N_KV_HEADS * HEAD_DIM
QKV_DIM = Q_DIM + 2 * KV_DIM
ALIBI_MAX_BIAS = 8.0

CHUNK = 128
SGU_HALF = 3 * D_MODEL
N_SGU_GROUPS = 8
SGU_GROUP_DIM = SGU_HALF // N_SGU_GROUPS

D_FF = 2816
CONV_WIDTH = 3


def rms_norm_2(x, g):
    xf = x.astype(jnp.float32)
    y = xf * lax.rsqrt(jnp.mean(xf * xf, axis=-1, keepdims=True) + EPS)
    return (y * g.astype(jnp.float32)).astype(x.dtype)

def layer_norm(x, g, b):
    xf = x.astype(jnp.float32)
    mu = jnp.mean(xf, axis=-1, keepdims=True)
    xc = xf - mu
    y = xc * lax.rsqrt(jnp.mean(xc * xc, axis=-1, keepdims=True) + EPS)
    return (y * g.astype(jnp.float32) + b.astype(jnp.float32)).astype(x.dtype)

def alibi_slopes():
    h = jnp.arange(1, N_HEADS + 1, dtype=jnp.float32)
    return jnp.exp2(-ALIBI_MAX_BIAS * h / N_HEADS)

def sliding_window_attention(h, w_qkv, b_qkv, sinks, w_o, b_o):
    B, S, _ = h.shape
    nb = S // BLOCK
    qkv = h @ w_qkv + b_qkv
    q, k, v = jnp.split(qkv, [Q_DIM, Q_DIM + KV_DIM], axis=-1)
    q = q.reshape(B, nb, BLOCK, N_KV_HEADS, Q_PER_KV, HEAD_DIM)
    k = k.reshape(B, nb, BLOCK, N_KV_HEADS, HEAD_DIM)
    v = v.reshape(B, nb, BLOCK, N_KV_HEADS, HEAD_DIM)

    def with_prev(t):
        prev = jnp.concatenate([jnp.zeros_like(t[:, :1]), t[:, :-1]], axis=1)
        return jnp.concatenate([prev, t], axis=2)

    kb, vb = with_prev(k), with_prev(v)
    scores = jnp.einsum("bnqgrd,bnkgd->bngrqk", q, kb).astype(jnp.float32) * (HEAD_DIM ** -0.5)

    qi = jnp.arange(BLOCK)[:, None]
    kj = jnp.arange(2 * BLOCK)[None, :]
    dist = qi + BLOCK - kj
    key_pos = jnp.arange(nb)[:, None, None] * BLOCK - BLOCK + kj[None]
    valid = (dist >= 0)[None] & (dist < WINDOW)[None] & (key_pos >= 0)

    slopes = alibi_slopes().reshape(N_KV_HEADS, Q_PER_KV)
    scores = scores - slopes[:, :, None, None] * dist.astype(jnp.float32)
    scores = jnp.where(valid[None, :, None, None], scores, -jnp.inf)

    sink = sinks.astype(jnp.float32).reshape(N_KV_HEADS, Q_PER_KV)[None, None, :, :, None, None]
    m = jnp.maximum(jnp.max(scores, axis=-1, keepdims=True), sink)
    p = jnp.exp(scores - m)
    probs = p / (jnp.sum(p, axis=-1, keepdims=True) + jnp.exp(sink - m))

    out = jnp.einsum("bngrqk,bnkgd->bnqgrd", probs.astype(h.dtype), vb)
    return out.reshape(B, S, Q_DIM) @ w_o + b_o

def chunked_sgu(h, w_in, ln_g, ln_b, w_s, b_s, w_out):
    B, S, _ = h.shape
    nc = S // CHUNK
    z = jax.nn.gelu(h @ w_in)
    u, v = jnp.split(z, 2, axis=-1)
    v = layer_norm(v, ln_g, ln_b)
    v = v.reshape(B, nc, CHUNK, N_SGU_GROUPS, SGU_GROUP_DIM)
    causal = jnp.tril(jnp.ones((CHUNK, CHUNK), dtype=bool))
    ws = jnp.where(causal[None], w_s, jnp.zeros_like(w_s))
    sv = jnp.einsum("gts,bcsgd->bctgd", ws, v) + b_s.T[None, None, :, :, None]
    return (u * sv.reshape(B, S, SGU_HALF)) @ w_out

def conv_gated_ffn(h, w_in, conv_w, conv_b, w_out):
    S = h.shape[1]
    g, u = jnp.split(h @ w_in, 2, axis=-1)
    gp = jnp.pad(g, ((0, 0), (CONV_WIDTH - 1, 0), (0, 0)))
    g = conv_b + sum(conv_w[k] * gp[:, k:k + S] for k in range(CONV_WIDTH))
    return (jax.nn.gelu(g) * u) @ w_out

def second_inputs(seed: int = 0) -> dict:
    key = jax.random.key(seed)
    ks = jax.random.split(key, 24)
    f32 = jnp.float32

    def nrm(k, shape, scale):
        return jax.random.normal(k, shape, f32) * scale

    nA, nB = N_ATTN_LAYERS, N_SGU_LAYERS
    return {
        "x": nrm(ks[0], (BATCH, SEQ, D_MODEL), 1.0),
        "attn_w_qkv": nrm(ks[1], (nA, D_MODEL, QKV_DIM), D_MODEL ** -0.5),
        "attn_b_qkv": nrm(ks[2], (nA, QKV_DIM), 0.02),
        "attn_sinks": nrm(ks[3], (nA, N_HEADS), 1.0),
        "attn_w_o": nrm(ks[4], (nA, Q_DIM, D_MODEL), Q_DIM ** -0.5),
        "attn_b_o": nrm(ks[5], (nA, D_MODEL), 0.02),
        "sgu_w_in": nrm(ks[6], (nB, D_MODEL, 2 * SGU_HALF), D_MODEL ** -0.5),
        "sgu_ln_g": 1.0 + nrm(ks[7], (nB, SGU_HALF), 0.05),
        "sgu_ln_b": nrm(ks[8], (nB, SGU_HALF), 0.02),
        "sgu_w_s": nrm(ks[9], (nB, N_SGU_GROUPS, CHUNK, CHUNK), CHUNK ** -0.5),
        "sgu_b_s": 1.0 + nrm(ks[10], (nB, N_SGU_GROUPS, CHUNK), 0.05),
        "sgu_w_out": nrm(ks[11], (nB, SGU_HALF, D_MODEL), SGU_HALF ** -0.5),
        "ffn_w_in": nrm(ks[12], (DEPTH, D_MODEL, 2 * D_FF), D_MODEL ** -0.5),
        "ffn_conv_w": nrm(ks[13], (DEPTH, CONV_WIDTH, D_FF), CONV_WIDTH ** -0.5),
        "ffn_conv_b": nrm(ks[14], (DEPTH, D_FF), 0.02),
        "ffn_w_out": nrm(ks[15], (DEPTH, D_FF, D_MODEL), D_FF ** -0.5),
        "norm_mix_pre": 1.0 + nrm(ks[16], (DEPTH, D_MODEL), 0.05),
        "norm_mix_post": 1.0 + nrm(ks[17], (DEPTH, D_MODEL), 0.05),
        "norm_ffn_pre": 1.0 + nrm(ks[18], (DEPTH, D_MODEL), 0.05),
        "norm_ffn_post": 1.0 + nrm(ks[19], (DEPTH, D_MODEL), 0.05),
    }

def second_block(x, attn_w_qkv, attn_b_qkv, attn_sinks, attn_w_o, attn_b_o,
              sgu_w_in, sgu_ln_g, sgu_ln_b, sgu_w_s, sgu_b_s, sgu_w_out,
              ffn_w_in, ffn_conv_w, ffn_conv_b, ffn_w_out,
              norm_mix_pre, norm_mix_post, norm_ffn_pre, norm_ffn_post):
    for i in range(DEPTH):
        j = i // N_MIXERS
        h = rms_norm_2(x, norm_mix_pre[i])
        if i % N_MIXERS == 0:
            h = sliding_window_attention(h, attn_w_qkv[j], attn_b_qkv[j], attn_sinks[j],
                                         attn_w_o[j], attn_b_o[j])
        else:
            h = chunked_sgu(h, sgu_w_in[j], sgu_ln_g[j], sgu_ln_b[j], sgu_w_s[j],
                            sgu_b_s[j], sgu_w_out[j])
        x = x + rms_norm_2(h, norm_mix_post[i])
        h = conv_gated_ffn(rms_norm_2(x, norm_ffn_pre[i]), ffn_w_in[i], ffn_conv_w[i],
                           ffn_conv_b[i], ffn_w_out[i])
        x = x + rms_norm_2(h, norm_ffn_post[i])
    return x


def setup_inputs(seed=0):
    out = dict(first_inputs(seed))
    for name, value in second_inputs(seed + 1).items():
        if name != "x":
            out[name + "_2"] = value
    return out


def reference(
    x, c, ctx, c_ctx, w_mod, b_mod, norm_pre, norm_post, w_in_even, lam_a, subln_a, conv_b,
    w_in_odd, rpb_c, w_out, attn_w_qkv_2, attn_b_qkv_2, attn_sinks_2, attn_w_o_2, attn_b_o_2,
    sgu_w_in_2, sgu_ln_g_2, sgu_ln_b_2, sgu_w_s_2, sgu_b_s_2, sgu_w_out_2, ffn_w_in_2,
    ffn_conv_w_2, ffn_conv_b_2, ffn_w_out_2, norm_mix_pre_2, norm_mix_post_2, norm_ffn_pre_2,
    norm_ffn_post_2,
):
    x = first_block(
        x, c, ctx, c_ctx, w_mod, b_mod, norm_pre, norm_post, w_in_even, lam_a, subln_a, conv_b,
        w_in_odd, rpb_c, w_out,
    )
    return second_block(
        x, attn_w_qkv_2, attn_b_qkv_2, attn_sinks_2, attn_w_o_2, attn_b_o_2, sgu_w_in_2,
        sgu_ln_g_2, sgu_ln_b_2, sgu_w_s_2, sgu_b_s_2, sgu_w_out_2, ffn_w_in_2, ffn_conv_w_2,
        ffn_conv_b_2, ffn_w_out_2, norm_mix_pre_2, norm_mix_post_2, norm_ffn_pre_2,
        norm_ffn_post_2,
    )


_drawn_inputs = setup_inputs


def setup_inputs(seed=0):
    import zlib

    import numpy as np

    out = dict(_drawn_inputs(seed))
    spreads = {}
    factors = {'lam_a': 8.0,
     'rpb_c': 6.061,
     'sgu_ln_g_2': 4.099,
     'sgu_ln_b_2': 8.0,
     'sgu_b_s_2': 2.931,
     'ffn_conv_b_2': 3.935}
    for name, (base, spread) in spreads.items():
        noise = np.random.default_rng([zlib.crc32(name.encode()), seed]).standard_normal(out[name].shape)
        drawn = base * np.exp(spread * noise) if base else spread * noise
        out[name] = __import__('jax').numpy.asarray(drawn.astype(out[name].dtype))
    for name, factor in factors.items():
        out[name] = (out[name] * factor).astype(out[name].dtype)
    return out
```

```python
import math
from contextlib import ExitStack

import numpy as np

import concourse.bass as bass
from concourse import mybir
from concourse.alu_op_type import AluOpType as ALU

ACT = mybir.ActivationFunctionType
AX = mybir.AxisListType.X
F32 = mybir.dt.float32
F32R = mybir.dt.float32r
ds = bass.ds

P = 128
D = 1024
KT = D // P
TX, TC = 512, 256
TA = TX + TC
WORK = 32768
A_HEADS, A_QK = 8, 32
N_HEADS, KV_HEADS, HD = 16, 4, 64
SWA_ORDER = [0, 2, 1, 3]
FF = 2816
FT = FF // P
SG = 3072
ST = SG // P
SG_GROUPS = 8
EPS = 1e-6
LAM0 = 0.8 - 0.6 * math.exp(0.0)
MASKED = -1e30

PARAMS = {}


def _params():
    at = 0
    for name, n in (("b_mod", 48), ("pre", 16), ("post", 16), ("conv_b", 12), ("subln", 1),
                    ("mix_pre", 16), ("mix_post", 16), ("ffn_pre", 16), ("ffn_post", 16),
                    ("b_qkv", 10), ("b_o", 8), ("cw0", 2 * FT), ("cw1", 2 * FT), ("cw2", 2 * FT),
                    ("cb", 2 * FT), ("ln_g", ST), ("ln_b", ST), ("cond", 16), ("b_v", 256),
                    ("sinks", 16), ("lam", 128)):
        PARAMS[name] = (at, n)
        at += n
    return at


N_PARAMS = _params()

PHASES = [("even", 16, 2048),
          ("out0", 4, 2048), ("odd", 12, 2048), ("out1", 4, 2048), ("qkv", 6, 2048),
          ("wo", 4, 2048), ("ffn0_in", 22, 2048), ("ffn0_out", 16, 1408),
          ("sgu_v", 12, 2048), ("sgu_u", 12, 2048), ("sgu_out", 16, 1536),
          ("ffn1_in", 22, 2048), ("ffn1_out", 16, 1408)]
MOD1_AFTER = [2, 3, 6, 7, 8, 9, 10, 11, 12, 13, 14, 15]
FIRST, WIDTH_OF = {}, []
for _name, _n, _w in PHASES:
    FIRST[_name] = len(WIDTH_OF)
    WIDTH_OF += [_w] * _n
N_PANELS = len(WIDTH_OF)


def build_kernel(nc, dram, out):
    with ExitStack() as ctx:
        def sem(name):
            return ctx.enter_context(nc.semaphore(name))

        def sb(name, shape):
            return ctx.enter_context(nc.sbuf_tensor(name, shape, F32))

        work_at = (nc.sbuf_base + 31) // 32 * 32
        sb("work", [P, WORK])
        x = sb("x", [P, KT, TX])
        raw = sb("raw", [P, 2, 2048])
        whi = sb("whi", [P, 2, 2048])
        wlo = sb("wlo", [P, 2, 2048])
        mats = sb("mats", [P, 4, P])
        ident, ones, blk, rot = (mats[:, i, :] for i in range(4))
        wave = sb("wave", [P, 2, 512])
        small = sb("small", [P, 256])
        mask64 = sb("mask64", [P, 64])
        pc = sb("pc", [P, N_PARAMS])
        cs = sb("cs", [P, 2, KT])
        modc = [sb(f"modc{i}", [P, 24, 2]) for i in range(2)]
        root = sb("root", [P, 6])
        hroot = sb("hroot", [P, 4, 6, 2])
        amul = sb("amul", [P, KT, 2])
        gmul = sb("gmul", [P, KT, 2])
        subl = sb("subl", [P, 1])
        eps = sb("eps", [P, 1])
        bq8 = sb("bq8", [P, 8])
        lam4 = sb("lam4", [P, 4])
        lam_t = sb("lam_t", [P, 64])
        temp = sb("temp", [P, 2304])
        late_at = (nc.sbuf_base + 31) // 32 * 32
        sb("late", [P, 2048])
        mraw = nc.alloc_sbuf_tensor_at("mraw", [P, 2048], F32, offset=late_at)
        wst = nc.alloc_sbuf_tensor_at("wst", [P, SG_GROUPS, P], F32, offset=late_at)
        bsb = nc.alloc_sbuf_tensor_at("bsb", [P, SG_GROUPS, P], F32, offset=late_at + 4096)
        stat = sb("stat", [P, 96])
        bns = sb("bns", [P, 4, 6, 6])
        ps = ctx.enter_context(nc.psum_tensor("ps", [P, 8, 512], F32))

        def place(name, at, shape, dtype=F32):
            return nc.alloc_sbuf_tensor_at(name, [P, *shape], dtype, offset=work_at + 4 * at)

        def parts(name, at, shape):
            return place(name, at, shape, F32R)

        def par(name, i, n=1):
            return pc[:, ds(PARAMS[name][0] + i, n)]

        h1hi, h1lo = parts("h1hi", 0, [KT, TA]), parts("h1lo", 6144, [KT, TA])
        cx = place("ctx", 12288, [KT, TC])
        A0 = 14336
        eq, ek = place("eq", A0, [4, TA]), place("ek", A0 + 3072, [4, TA])
        ev = place("ev", A0 + 6144, [6, 512])
        hwide = place("hwide", A0, [4, 6, P])
        ega, eob, eot = (place(k, A0 + 9216 + i * 3072, [4, TA]) for i, k in enumerate(("ega", "eob", "eot")))
        zpad = place("zpad", A0 + 15360, [776])
        ycv = place("ycv", A0 + 16200, [776])
        sgb = place("sgb", A0 + 17000, [TA])
        y1 = place("y1", A0, [KT, TA])
        mod_w = [place("mod_w0", 0, [6, 2048]), place("mod_w1", A0, [6, 2048])]
        rows_t = place("rows", A0 + 17800, [512])
        rows = [rows_t[0:2, i * 256:(i + 1) * 256] for i in range(2)]
        atx = [place(f"atx{i}", i * 3072, [6, 512]) for i in range(2)]
        atc = [place(f"atc{i}", 6144 + i * 512, [2, 256]) for i in range(2)]
        prob = [place(f"prob{i}", 7168 + i * 1536, [2, TA]) for i in range(3)]
        prob.append(temp[:, 0:2 * TA].rearrange("p (m n) -> p m n", m=2))
        oprob = [place(f"oprob{i}", 7168 + i * 768, [TA]) for i in range(4)]
        oq, ok = place("oq", A0, [4, TX]), place("ok", A0 + 2048, [4, TA])
        ov = place("ov", A0 + 5120, [6, 512])
        ogn, ogd, oud, oot = (place(k, A0 + 8192 + i * 2048, [4, TX]) for i, k in enumerate(("ogn", "ogd", "oud", "oot")))
        o1hi, o1lo = parts("o1hi", 0, [KT, TX]), parts("o1lo", 4096, [KT, TX])
        dft = place("dft", 0, [2, 4, TX])
        four = place("four", 4096, [4, 1024])
        bias_t = [place(f"bias_t{i}", 10240 + i * 960, [15, 64]) for i in range(2)]
        h2hi, h2lo = parts("h2hi", 0, [KT, TX]), parts("h2lo", 4096, [KT, TX])
        y2, ywo = place("y2", 0, [KT, TX]), place("ywo", 8192, [KT, TX])
        mhi, mlo = parts("mhi", 8192, [ST, TX]), parts("mlo", 20480, [ST, TX])
        vtok = place("vtok", 20480, [ST, 4, P])
        sq8 = place("sq8", 8192, [8, TX])
        sk2, skd = place("sk2", 12288, [2, TX]), place("skd", 13312, [4, TX])
        sv = place("sv", 15360, [4, 256])
        alibi = place("alibi", 16384, [N_HEADS, 256])
        sprob = [place(f"sprob{i}", 20480 + i * 1024, [4, 256]) for i in range(4)]
        spt = [place(f"spt{i}", 29696 + i * 1024, [2, 512]) for i in range(2)]
        so = place("so", 25600, [8, TX])

        sq = [temp[:, i * TA:(i + 1) * TA] for i in range(2)]
        acc = temp[:, 2 * TA:3 * TA]
        rx, rc, sums = ps[:, 7, :], ps[:, 6, TC:2 * TC], ps[:, 6, 48:54]
        tap = [temp[:, i * 512:(i + 1) * 512] for i in range(2)]
        gel = [temp[:, 1024 + i * 512:1024 + (i + 1) * 512] for i in range(2)]
        ug = [temp[:, i * 1024:(i + 1) * 1024].rearrange("p (j n) -> p j n", j=2) for i in range(2)]

        raw_loaded = [sem("raw_loaded0"), sem("raw_loaded1")]
        split_done = sem("split_done")
        panel_done = sem("panel_done")
        params_in, consts_in, x_in, out_done = sem("params_in"), sem("consts_in"), sem("x_in"), sem("out_done")
        dve_order, act_order = sem("dve_order"), sem("act_order")
        mod_rows, mod_cols = sem("mod_rows"), sem("mod_cols")
        cond_ready = sem("cond_ready")
        mod_ready = sem("mod_ready")
        NORMS = ["pre0", "post0", "pre1", "post1", "mixpre0", "mixpost0", "ffnpre0", "ffnpost0",
                 "mixpre1", "mixpost1", "ffnpre1", "ffnpost1"]
        NORM = {k: i for i, k in enumerate(NORMS)}
        n_sq = sem("norm_squares")
        n_acc = sem("norm_added")
        n_mm = sem("norm_summed")
        n_rt = sem("norm_root")
        n_full = {k: sem(f"{k}_full") for k in NORMS}
        n_hi = {k: sem(f"{k}_hi") for k in NORMS}
        n_ok = {k: sem(f"{k}_done") for k in NORMS}
        e_free, zed, cb_in, sg_in, b_free = (sem(n) for n in ("e_free", "z_made", "cb_copied",
                                                              "gate_b_made", "b_made"))
        rot_mm, rot_done = sem("rotated"), sem("rope_done")
        mod_in, mod1_in, mod_used, late_in = ([sem(f"mod_in{i}") for i in range(6)], sem("mod1_in"),
                                                sem("mod_used"), sem("late_in"))
        ea = {k: sem(f"even_{k}") for k in ("scores", "negmax", "exp", "probs", "transposed",
                                            "copied", "pv", "out", "zeroed", "hi", "lo", "sq", "sums", "root", "inverse", "spread",
                                            "normed", "mixed", "lam", "lam_exp")}
        oa = {k: sem(f"odd_{k}") for k in ("scores", "negmax", "exp", "probs", "transposed",
                                           "copied", "pv", "out", "zeroed", "hi", "lo", "bias_in", "bias", "mixed",
                                           "biased")}
        o_free = sem("odd_free")
        fo = {k: sem(f"fourier_{k}") for k in ("const", "half", "copied", "full", "out")}
        y_free = {k: sem(f"{k}_free") for k in ("out0", "out1", "wo", "ffn0_out", "sgu_out", "ffn1_out")}
        q_free, v_free, kdup = sem("qk_copied"), sem("v_copied"), sem("k_doubled")
        alibi_ready, dist_in = sem("alibi_ready"), sem("dist_in")
        swa_even = sem("swa_even_heads")
        sa = {k: sem(f"swa_{k}") for k in ("scores", "negmax", "exp", "probs", "transposed",
                                           "copied", "pv", "out", "hi", "lo", "mixed")}
        ff = [{k: sem(f"ffn{i}_{k}") for k in ("tap", "taps", "gelu", "gated")} for i in range(2)]
        sg = {k: sem(f"sgu_{k}") for k in ("v", "moments", "root", "normed", "gelu", "gated",
                                           "rowsum", "ws", "rows_copied", "uhalf")}

        block = ctx.enter_context(nc.Block())

        def mod_bank(layer, k):
            return ps[0:2, 5 if layer == 0 and k < 8 else 7, 0:256]

        @block.sync
        def _(sp):
            sp.dma_start(pc[:], dram["params"]).then_inc(params_in, 16)
            sp.dma_start(x[:], dram["xT"]).then_inc(x_in, 16)
            sp.dma_start(cx[:], dram["ctxT"]).then_inc(x_in, 16)
            sp.dma_start(mats[:], dram["mats"]).then_inc(params_in, 16)

            def load(phase, k, n, slot, width):
                if not isinstance(n, int) or n >= 2:
                    sp.wait_ge(split_done, n - 1)
                sp.dma_start(raw[:, slot, 0:width], dram[phase][ds(k, 1), :, :].rearrange("k p n -> (k p) n"))\
                    .then_inc(raw_loaded[slot], 16)

            def load_mod0(i):
                sp.dma_start(mod_w[i // 3][:, 2 * (i % 3):2 * (i % 3) + 2, :],
                             dram["mod0"][2 * i:2 * i + 2, :, :].rearrange("k p n -> p k n")).then_inc(mod_in[i], 16)

            for i in range(4):
                load_mod0(i)
            for k in range(2):
                load("even", k, k, k, 2048)
            for i in range(4, 6):
                load_mod0(i)
            sp.dma_start(wave[:], dram["wave"]).then_inc(consts_in, 16)
            sp.dma_start(small[:], dram["dft64"]).then_inc(consts_in, 16)
            sp.dma_start(mask64[:], dram["mask64"]).then_inc(consts_in, 16)
            for e in range(2, 16):
                load("even", e, e, e % 2, 2048)
                if e in MOD1_AFTER:
                    m = MOD1_AFTER.index(e)
                    if m:
                        sp.wait_ge(mod_used, 12 + m)
                    sp.dma_start(mraw[:], dram["mod1"][m, :, :]).then_inc(mod1_in, 16)
            sp.wait_ge(mod_used, 24)
            sp.dma_start(wst[:], dram["wsT"]).then_inc(late_in, 16)
            sp.dma_start(bsb[:], dram["bs"]).then_inc(late_in, 16)
            for phase, count, width in PHASES[1:]:
                p0 = FIRST[phase]
                with sp.Fori(0, count // 2) as i:
                    for slot in range(2):
                        load(phase, 2 * i + slot, p0 + 2 * i + slot, slot, width)
            sp.wait_ge(n_ok["ffnpost1"], 8)
            sp.dma_start(out, x[:]).then_inc(out_done, 16)
            sp.wait_ge(out_done, 16)

        @block.tensor
        def _(pe):
            def r(ap):
                return ap.bitcast(F32R)

            def mm3(o, lhi, llo, rhi, rlo, first, last):
                pe.matmul(o, r(lhi), r(rhi), start=first, stop=False)
                pe.matmul(o, r(lhi), r(rlo), start=False, stop=False)
                return pe.matmul(o, r(llo), r(rhi), start=False, stop=last)

            def w(slot, hl, kt, width=256, at=0, n=P):
                return (whi, wlo)[hl][:, slot, kt * width + at:kt * width + at + n]

            def feature_panel(slot, n, banks, cbank, hi, lo, parts_made=None, kts=range(KT)):
                pe.wait_ge(split_done, n + 1)
                def x_part(j, i):
                    kt = kts[i]
                    return mm3(ps[:, banks[j], :], w(slot, 0, kt, at=j * P), w(slot, 1, kt, at=j * P),
                               hi[:, kt, 0:TX], lo[:, kt, 0:TX], i == 0, i == KT - 1)

                def ctx_part(j, i):
                    kt = kts[i]
                    return mm3(ps[:, cbank, j * TC:(j + 1) * TC], w(slot, 0, kt, at=j * P), w(slot, 1, kt, at=j * P),
                               hi[:, kt, TX:TA], lo[:, kt, TX:TA], i == 0, i == KT - 1)

                if parts_made is not None:
                    for i in range(KT):
                        pe.wait_ge(parts_made, i + 1)
                        x_part(0, i)
                        if cbank is not None:
                            ctx_part(0, i)
                        last = x_part(1, i)
                    for i in range(KT if cbank is not None else 0):
                        last = ctx_part(1, i)
                else:
                    for j in range(2):
                        for i in range(KT):
                            last = x_part(j, i)
                            if cbank is not None:
                                last = ctx_part(j, i)
                last.then_inc(panel_done, 1)

            def token_panel(slot, n, bank, tiles, hi, lo, parts_made=None):
                pe.wait_ge(split_done, n + 1)
                for t in range(tiles):
                    for kt in range(KT):
                        if parts_made is not None and t == 0:
                            pe.wait_ge(parts_made, kt + 1)
                        last = mm3(ps[:, bank + t // 2, t % 2 * 256:t % 2 * 256 + 256],
                                   hi[:, kt, t * P:(t + 1) * P], lo[:, kt, t * P:(t + 1) * P],
                                   w(slot, 0, kt, n=256), w(slot, 1, kt, n=256), kt == 0, kt == KT - 1)
                last.then_inc(panel_done, 1)

            def mod_panel(layer, k):
                if layer == 0:
                    pe.wait_ge(mod_in[k // 2], 16)
                    panel = mod_w[k // 6][:, k % 6, :]
                else:
                    pe.wait_ge(mod1_in, 16 * (k + 1))
                    panel = mraw[:, :]
                if k + 12 * layer:
                    pe.wait_ge(mod_rows, 12 * layer + k)
                for kt in range(KT):
                    last = pe.matmul(mod_bank(layer, k), cs[:, :, kt], panel[:, kt * 256:(kt + 1) * 256],
                                     start=kt == 0, stop=kt == KT - 1)
                last.then_inc(mod_used, 1)

            def mod_columns(layer, k):
                pe.wait_ge(mod_rows, 12 * layer + k + 1)
                for j in range(2):
                    at = 64 * layer + 4 * k + 2 * j
                    last = pe.matmul(ps[:, 6, at:at + 2], rows[k % 2][:, j * P:(j + 1) * P], ident[0:2, 0:2],
                                     start=True, stop=True)
                last.then_inc(mod_cols, 1)

            def norm_sums(key, ctx_too):
                tiles = 6 if ctx_too else 4
                pe.wait_ge(n_acc, (KT + 1) * NORM[key] + 1 + KT)
                for t in range(tiles):
                    last = pe.matmul(ps[:, 6, 48 + t:49 + t], acc[:, t * P:(t + 1) * P], ones[:, 0:1],
                                     start=True, stop=True)
                last.then_inc(n_mm, 1)
                pe.wait_ge(n_rt, 2 * NORM[key] + 2)
                for t in range(tiles):
                    o = rx[:, t * P:(t + 1) * P] if t < 4 else rc[:, (t - 4) * P:(t - 3) * P]
                    last = pe.matmul(o, root[:, t:t + 1].broadcast_to([P, P]), ident, start=True, stop=True)
                last.then_inc(n_mm, 1)

            def transposed(o, in_):
                return pe.transpose(o, in_, ident)

            pe.wait_ge(params_in, 32)
            pe.wait_ge(cond_ready, 2)
            mod_panel(0, 0)
            norm_sums("pre0", True)
            for k in range(8):
                if k:
                    mod_panel(0, k)
                if k:
                    mod_columns(0, k - 1)
            mod_columns(0, 7)

            def even_panel(e):
                s = e % 2
                if e in (4, 6, 8):
                    pe.wait_ge(e_free, e)
                elif e >= 10:
                    pe.wait_ge((zed, b_free)[s], (e - 8) // 2)
                elif e in (2, 3):
                    pe.wait_ge(e_free, e - 1)
                if e in (4, 5):
                    token_panel(s, e, 3 * s, 6, h1hi, h1lo)
                else:
                    feature_panel(s, e, (2 * s, 2 * s + 1), 4 + s, h1hi, h1lo, n_ok["pre0"] if e == 0 else None)

            even_panel(0)
            even_panel(1)
            pe.wait_ge(mod_ready, 2)
            for k in range(8, 12):
                mod_panel(0, k)
                mod_columns(0, k)
            for e in range(2, 16):
                even_panel(e)
                if e in MOD1_AFTER:
                    m = MOD1_AFTER.index(e)
                    if m == 1:
                        pe.wait_ge(mod_ready, 4)
                    if m:
                        mod_columns(1, m - 1)
                    mod_panel(1, m)
            mod_columns(1, 11)
            def stacked_product(o, slot, q_at, width, k_at, n):
                q = r(whi[:, slot, q_at:q_at + P])
                pe.matmul(o, q, r(wlo[:, slot, k_at:k_at + n]), start=True, stop=False)
                return pe.matmul(o, q, r(wlo[:, slot, width + k_at:width + k_at + n]), start=False, stop=True)

            pe.wait_ge(b_free, 4)
            for t in range(8):
                if t >= 2:
                    pe.wait_ge(rot_done, t - 1)
                src = (eq, ek)[t // 4]
                pe.matmul(ps[:, t % 2, :], rot, src[:, t % 4, 0:TX], start=True, stop=True).then_inc(rot_mm, 1)
            pe.wait_ge(rot_done, 8)

            units = [(h, t) for h in range(A_HEADS) for t in range(6)]

            def even_scores(v):
                h, t = units[v // 2]
                m, b = v % 2, 2 * (v % 2)
                if v % 12 == 0:
                    pe.wait_ge(ea["lo"], 3 * (h + 1))
                if v >= 2:
                    pe.wait_ge(ea["exp"], v - 1)
                if t < 4:
                    stacked_product(ps[:, b, :], h % 2, m * TA + t * P, TA, 0, TX)
                    last = stacked_product(ps[:, b + 1, 0:TC], h % 2, m * TA + t * P, TA, TX, TC)
                else:
                    last = stacked_product(ps[:, b, 0:TC], h % 2, m * TA + t * P, TA, TX, TC)
                last.then_inc(ea["scores"], 1)

            def even_pv(h, part):
                if part == 0:
                    pe.wait_ge(ea["copied"], 6 * h + 6)
                    if h >= 1:
                        pe.wait_ge(ea["out"], h)
                if part < 3:
                    for kt in range(2 * part, 2 * part + 2):
                        pe.matmul(ps[0:64, 6, :], ev[:, kt, h * 64:h * 64 + 64], atx[h % 2][:, kt, :],
                                  start=kt == 0, stop=kt == 5)
                    return
                for kt in range(2):
                    last = pe.matmul(ps[0:64, 7, 0:TC], ev[:, 4 + kt, h * 64:h * 64 + 64], atc[h % 2][:, kt, :],
                                     start=kt == 0, stop=kt == 1)
                last.then_inc(ea["pv"], 1)

            for v in range(6):
                even_scores(v)
            for u, (h, t) in enumerate(units):
                if u + 3 < len(units):
                    even_scores(2 * u + 6)
                    even_scores(2 * u + 7)
                pe.wait_ge(ea["probs"], u + 1)
                if u >= 1:
                    pe.wait_ge(ea["copied"], u)
                for kt in range(6 if t < 4 else 2):
                    last = transposed(ps[:, 4 + kt // 4, kt % 4 * P:kt % 4 * P + P],
                                      prob[u % 4][:, 0, kt * P:(kt + 1) * P])
                last.then_inc(ea["transposed"], 1)
                if 1 <= t <= 4 and h:
                    even_pv(h - 1, t - 1)
            for part in range(4):
                even_pv(A_HEADS - 1, part)
            for t in range(4):
                pe.wait_ge(ea["sq"], t + 1)
                for c in range(6):
                    last = pe.matmul(ps[:, 4, 16 * t + 2 * c:16 * t + 2 * c + 2], sq[t % 2][:, c * P:(c + 1) * P],
                                     blk[:, 0:P:64], start=True, stop=True)
                last.then_inc(ea["sums"], 1)
            for t in range(4):
                pe.wait_ge(ea["inverse"], t + 1)
                if t >= 2:
                    pe.wait_ge(ea["normed"], t - 1)
                b = (6, 2)[t % 2]
                for c in range(6):
                    last = pe.matmul(ps[:, b + c // 4, c % 4 * P:c % 4 * P + P],
                                     hwide[:, t, c, :], ident,
                                     start=True, stop=True)
                last.then_inc(ea["spread"], 1)

            def out_projection(phase, norm, ctx_too, hi, lo, parts_made, kts=range(KT)):
                p0 = FIRST[phase]
                for k in range(4):
                    s = k % 2
                    if k >= 2:
                        pe.wait_ge(y_free[phase], k - 1)
                        pe.wait_ge(n_sq, KT * NORM[norm] + 2 * (k - 1))
                    feature_panel(s, p0 + k, (2 * s, 2 * s + 1), 4 + s if ctx_too else None, hi, lo,
                                  parts_made if k == 0 else None, kts)

            out_projection("out0", "post0", True, h1hi, h1lo, ea["mixed"], (4, 5, 6, 7, 0, 1, 2, 3))
            norm_sums("post0", True)
            norm_sums("pre1", True)

            p0 = FIRST["odd"]
            for k in range(12):
                b, s = k // 2, k % 2
                if k in (4, 6):
                    pe.wait_ge(o_free, k)
                elif k >= 2 and k not in (5, 7):
                    pe.wait_ge(o_free, k - 1)
                if b == 2:
                    token_panel(s, p0 + k, 3 * s, 6, h1hi, h1lo)
                else:
                    feature_panel(s, p0 + k, (2 * s, 2 * s + 1), 4 + s if b == 1 else None, h1hi, h1lo,
                                  n_ok["pre1"] if k == 0 else None)
            pe.wait_ge(o_free, 12)
            n = 0
            for t in range(4):
                for f in range(4):
                    if n >= 8:
                        pe.wait_ge(fo["copied"], n // 2 - 3)
                    last = pe.matmul(ps[:, n // 2 % 4, n % 2 * 256:n % 2 * 256 + 256], oud[:, f, t * P:(t + 1) * P],
                                     small[:, :], start=True, stop=True)
                    last.then_inc(fo["half"], 1)
                    n += 1
            pe.wait_ge(fo["const"], 16)
            pe.wait_ge(fo["copied"], 8)
            for f in range(4):
                for t in range(4):
                    for c in range(2):
                        last = pe.matmul(ps[:, 4 + f, :], four[:, t, f * 256 + c * P:f * 256 + c * P + P],
                                         dft[:, c, t, :], start=t == 0 and c == 0, stop=t == 3 and c == 1)
                last.then_inc(fo["full"], 1)
            pe.wait_ge(fo["out"], 4)

            def odd_scores(u):
                h, t = u // 4, u % 4
                b = 2 * (u % 2)
                if t == 0:
                    pe.wait_ge(oa["lo"], 2 * (h + 1))
                if u >= 2:
                    pe.wait_ge(oa["exp"], u - 1)
                stacked_product(ps[:, b, :], h % 2, t * P, TA, 0, TX)
                stacked_product(ps[:, b + 1, 0:TC], h % 2, t * P, TA, TX, TC).then_inc(oa["scores"], 1)

            def odd_pv(h, part):
                if part == 0:
                    pe.wait_ge(oa["copied"], 4 * h + 4)
                    if h >= 1:
                        pe.wait_ge(oa["out"], h)
                for kt in range(2 * part, 2 * part + 2):
                    last = pe.matmul(ps[0:64, 6, :], ov[:, kt, h * 64:h * 64 + 64], atx[h % 2][:, kt, :],
                                     start=kt == 0, stop=kt == 5)
                if part == 2:
                    last.then_inc(oa["pv"], 1)

            odd_scores(0)
            odd_scores(1)
            odd_scores(2)
            for u in range(32):
                if u + 3 < 32:
                    odd_scores(u + 3)
                pe.wait_ge(oa["probs"], u + 1)
                if u >= 1:
                    pe.wait_ge(oa["copied"], u)
                for kt in range(6):
                    last = transposed(ps[:, 4 + kt // 4, kt % 4 * P:kt % 4 * P + P],
                                      oprob[u % 4][:, kt * P:(kt + 1) * P])
                last.then_inc(oa["transposed"], 1)
                if u % 4 >= 1 and u > 4:
                    odd_pv(u // 4 - 1, u % 4 - 1)
            for part in range(3):
                odd_pv(7, part)
            out_projection("out1", "post1", False, o1hi, o1lo, oa["mixed"], (4, 5, 6, 7, 0, 1, 2, 3))
            norm_sums("post1", False)

            norm_sums("mixpre0", False)
            p0 = FIRST["qkv"]
            for k in range(5):
                s = k % 2
                if k >= 2:
                    pe.wait_ge(q_free, k - 1)
                feature_panel(s, p0 + k, (2 * s, 2 * s + 1), None, h2hi, h2lo, n_ok["mixpre0"] if k == 0 else None)
            token_panel(1, p0 + 5, 6, 4, h2hi, h2lo)
            pe.wait_ge(kdup, 8)

            def swa_scores(u):
                g, n = u // 4, u % 4
                if u >= 2:
                    pe.wait_ge(sa["exp"], 5 * (u - 1))
                k0 = 0 if n else P
                if n == 0:
                    pe.wait_ge(sa["lo"], 3 * (g + 1))
                for q in range(4):
                    last = stacked_product(ps[:, 2 * (u % 2) + q // 2, q % 2 * 256 + k0:q % 2 * 256 + 256],
                                           g % 2, q * TX + n * P, TX, (n - 1) * P + k0, 2 * P - k0)
                last.then_inc(sa["scores"], 1)

            def swa_pv(u):
                g, n = u // 4, u % 4
                pe.wait_ge(sa["copied"], u + 1)
                if u >= 2:
                    pe.wait_ge(sa["out"], u - 1)
                for kt in range(0 if n else 1, 2):
                    last = pe.matmul(ps[0:64, 6 + u % 2, :], sv[:, n - 1 + kt, g * 64:g * 64 + 64],
                                     spt[u % 2][:, kt, :], start=kt == (0 if n else 1), stop=kt == 1)
                last.then_inc(sa["pv"], 1)

            pe.wait_ge(v_free, 1)
            swa_scores(0)
            swa_scores(1)
            swa_scores(2)
            for u in range(16):
                if u + 3 < 16:
                    swa_scores(u + 3)
                pe.wait_ge(sa["probs"], u + 1)
                if u >= 1:
                    pe.wait_ge(sa["copied"], u)
                for kt in range(0 if u % 4 else 1, 2):
                    for q in range(4):
                        last = transposed(ps[:, 4 + kt, q * P:(q + 1) * P],
                                          sprob[u % 4][:, q, kt * P:(kt + 1) * P])
                last.then_inc(sa["transposed"], 1)
                if u:
                    swa_pv(u - 1)
            swa_pv(15)
            out_projection("wo", "mixpost0", False, h2hi, h2lo, sa["mixed"])
            norm_sums("mixpost0", False)

            def ffn(layer):
                f = ff[layer]
                p0 = FIRST[f"ffn{layer}_in"]
                norm_sums(f"ffnpre{layer}", False)
                for s in range(2):
                    feature_panel(s, p0 + s, (2 * s, 2 * s + 1), None, h2hi, h2lo,
                                  n_ok[f"ffnpre{layer}"] if s == 0 else None)
                with pe.Fori(1, 11) as i:
                    for s in range(2):
                        pe.wait_ge(f["gated"], 2 * i + s - 1)
                        feature_panel(s, p0 + 2 * i + s, (2 * s, 2 * s + 1), None, h2hi, h2lo)
                pe.wait_ge(f["gated"], FT)
                long_out(f"ffn{layer}_out", f"ffnpost{layer}", FT // 2)
                norm_sums(f"ffnpost{layer}", False)

            def long_out(phase, norm, kts):
                p0 = FIRST[phase]

                def pair(i, first):
                    for j in range(2):
                        if not first:
                            pe.wait_ge(y_free[phase], 2 * i + j - 1)
                            pe.wait_ge(n_sq, KT * NORM[norm] + 2 * i + j - 1)
                        for s in range(2):
                            pe.wait_ge(split_done, p0 + 4 * i + 2 * j + s + 1)
                            for kt in range(kts):
                                last = mm3(ps[:, j, :], w(s, 0, kt, width=P), w(s, 1, kt, width=P),
                                           mhi[:, s * kts + kt, :], mlo[:, s * kts + kt, :],
                                           s == 0 and kt == 0, s == 1 and kt == kts - 1)
                            last.then_inc(panel_done, 1)
                pair(0, True)
                with pe.Fori(1, 4) as i:
                    pair(i, False)

            ffn(0)
            norm_sums("mixpre1", False)
            p0 = FIRST["sgu_v"]
            for s in range(2):
                token_panel(s, p0 + s, 2 * s, 4, h2hi, h2lo, n_ok["mixpre1"] if s == 0 else None)
            with pe.Fori(1, 6) as i:
                for s in range(2):
                    pe.wait_ge(sg["v"], 2 * (2 * i + s - 1))
                    token_panel(s, p0 + 2 * i + s, 2 * s, 4, h2hi, h2lo)
            pe.wait_ge(sg["ws"], 1)
            for g in range(SG_GROUPS):
                last = pe.matmul(ps[:, 4 + g // 4, g % 4 * P:g % 4 * P + P], ones, wst[:, g, :], start=True, stop=True)
            last.then_inc(sg["rowsum"], 1)
            pe.wait_ge(sg["rows_copied"], 2)
            pe.wait_ge(sg["v"], 24)
            p0 = FIRST["sgu_u"]
            for k in range(12):
                s = k % 2
                if k >= 2:
                    pe.wait_ge(sg["gelu"], k - 1)
                feature_panel(s, p0 + k, (2 * s, 2 * s + 1), None, h2hi, h2lo)
                if k == 0:
                    pe.wait_ge(sg["normed"], 4)
                if k >= 2:
                    pe.wait_ge(sg["gated"], 2 * (k - 1))
                for j in range(2):
                    dt = 2 * k + j
                    for c in range(4):
                        last = pe.matmul(ps[:, 4 + 2 * s + j, c * P:(c + 1) * P], vtok[:, dt, c, :],
                                         wst[:, dt // 3, :], start=True, stop=True)
                last.then_inc(sg["uhalf"], 1)
            pe.wait_ge(sg["gated"], ST)
            long_out("sgu_out", "mixpost1", ST // 2)
            norm_sums("mixpost1", False)
            ffn(1)

        @block.scalar
        def _(act):
            order = [0, 0]

            def step(ins):
                order[1] += 1
                ins.then_inc(act_order, 1)
                act.wait_ge(act_order, order[0] + order[1])

            def tell(ins, done, value):
                ins.then_inc(done, 1)
                act.wait_ge(done, value)

            def copy(o, in_, func=ACT.Identity, **kw):
                return act.activation(o, in_, func, **kw)

            def square(key, kt, src, csrc=None, **kw):
                if not isinstance(kt, int) or kt >= 2:
                    act.wait_ge(n_acc, (KT + 1) * NORM[key] + kt)
                if csrc is not None:
                    step(copy(sq[kt % 2][:, TX:TA], csrc, ACT.Square))
                copy(sq[kt % 2][:, 0:TX], src, ACT.Square, **kw).then_inc(n_sq, 1)

            def norm_root(key, ctx_too):
                act.wait_ge(n_mm, 2 * NORM[key] + 1)
                tiles = 6 if ctx_too else 4
                tell(copy(root[:, 0:tiles], sums[:, 0:tiles], ACT.Sqrt, bias=eps[:, 0:1], scale=1.0 / D),
                     n_rt, 2 * NORM[key] + 1)

            def pre_norm(key, ctx_too, after=None):
                for kt in range(KT):
                    if after is not None:
                        act.wait_ge(n_ok[after], kt + 1)
                    square(key, kt, x[:, kt, :], cx[:, kt, :] if ctx_too else None)
                norm_root(key, ctx_too)

            def hi_parts(key, hi, layer=None):
                for kt in range(KT):
                    full = sq[kt % 2]
                    if layer is None:
                        act.wait_ge(n_full[key], kt + 1)
                        copy(hi[:, kt, 0:TX], full[:, 0:TX]).then_inc(n_hi[key], 1)
                    else:
                        act.wait_ge(n_full[key], 2 * (kt + 1))
                        copy(hi[:, kt, TX:TA], full[:, TX:TA], bias=modc[layer][:, kt, 1:2]).then_inc(n_hi[key], 1)
                        copy(hi[:, kt, 0:TX], full[:, 0:TX], bias=modc[layer][:, kt, 0:1]).then_inc(n_hi[key], 1)

            def mod_row(layer, k):
                n = 12 * layer + k
                act.wait_ge(mod_used, n + 1)
                if n >= 2:
                    act.wait_ge(mod_cols, n - 1)
                copy(rows[k % 2], mod_bank(layer, k)).then_inc(mod_rows, 1)

            act.wait_ge(params_in, 32)
            act.wait_ge(cond_ready, 1)
            copy(cs[:], pc[:, PARAMS["cond"][0]:PARAMS["cond"][0] + 16].rearrange("p (a k) -> p a k", a=2),
                 ACT.Silu).then_inc(cond_ready, 1)
            act.wait_ge(x_in, 32)
            pre_norm("pre0", True)
            for k in range(8):
                mod_row(0, k)
            hi_parts("pre0", h1hi, 0)

            def features_out(n, s, o, co, func=ACT.Identity, scale=1.0):
                act.wait_ge(panel_done, n + 1)
                step(copy(co, ps[:, 4 + s, :].rearrange("p (j n) -> p j n", j=2), func, scale=scale))
                return copy(o, ps[:, 2 * s:2 * s + 2, :], func, scale=scale)

            for e in range(8):
                s = e % 2
                if e // 2 == 2:
                    act.wait_ge(panel_done, e + 1)
                    last = copy(ev[:, :, s * 256:(s + 1) * 256].rearrange("p (b t) n -> p b t n", t=2),
                                ps[:, 3 * s:3 * s + 3, :].rearrange("p b (t n) -> p b t n", t=2))
                else:
                    dst = (eq, ek, None, ega)[e // 2][:, 2 * s:2 * s + 2, :]
                    last = features_out(e, s, dst[:, :, 0:TX], dst[:, :, TX:TA],
                                        ACT.Silu if e // 2 == 3 else ACT.Identity,
                                        A_QK ** -0.5 if e // 2 == 0 else 1.0)
                tell(last, e_free, e + 1)
                if e == 1:
                    for k in range(8, 12):
                        mod_row(0, k)
                if e in MOD1_AFTER:
                    mod_row(1, MOD1_AFTER.index(e))
            for j in range(4):
                e = 8 + 2 * j
                act.wait_ge(panel_done, e + 1)
                step(copy(eob[:, j, TX:TA], ps[:, 4, 0:TC]))
                tell(copy(eob[:, j, 0:TX], ps[:, 0, :]), cb_in, j + 1)
                mod_row(1, MOD1_AFTER.index(e))
                act.wait_ge(panel_done, e + 2)
                if j:
                    act.wait_ge(b_free, j)
                step(copy(sgb[:, TX:TA], ps[:, 5, TC:2 * TC], ACT.Silu))
                tell(copy(sgb[:, 0:TX], ps[:, 3, :], ACT.Silu), sg_in, j + 1)
                mod_row(1, MOD1_AFTER.index(e + 1))
            act.wait_ge(ea["lam"], 1)
            tell(copy(lam4[:, 0:2], lam4[:, 0:2], ACT.Exp), ea["lam_exp"], 1)

            units = [(h, t) for h in range(A_HEADS) for t in range(6)]

            def even_exp(v):
                u, m = v // 2, v % 2
                n = TA if units[u][1] < 4 else TC
                act.wait_ge(ea["negmax"], v + 1)
                if u >= 4:
                    act.wait_ge(ea["transposed"], u - 3)
                scr = ps[:, 2 * m:2 * m + 2, :].rearrange("p b n -> p (b n)")
                act.activation(prob[u % 4][:, m, 0:n], scr[:, 0:n], ACT.Exp, bias=stat[:, v % 8:v % 8 + 1],
                               accum_out=stat[:, 8 + v % 8:9 + v % 8]).then_inc(ea["exp"], 1)

            def even_copy(u):
                h, t = units[u]
                act.wait_ge(ea["transposed"], u + 1)
                if h >= 2:
                    act.wait_ge(ea["pv"], h - 1)
                flat = ps[:, 4:6, :].rearrange("p b (k n) -> p (b k) n", n=P)
                if t < 4:
                    copy(atx[h % 2][:, :, t * P:(t + 1) * P], flat[:, 0:6, :]).then_inc(ea["copied"], 1)
                else:
                    copy(atc[h % 2][:, :, (t - 4) * P:(t - 3) * P], flat[:, 0:2, :]).then_inc(ea["copied"], 1)

            def even_out(h):
                act.wait_ge(ea["pv"], h + 1)
                o = eot[h % 2 * 64:h % 2 * 64 + 64, h // 2, :]
                step(copy(o[:, 0:TX], ps[0:64, 6, :]))
                tell(copy(o[:, TX:TA], ps[0:64, 7, 0:TC]), ea["out"], h + 1)

            def even_hi(h, part):
                a, s, t = h % 2 * 64, h % 2, h // 2
                if h >= 2:
                    act.wait_ge(ea["scores"], 12 * (h - 1))
                for m in range(2):
                    if part == 0:
                        r0 = a + 32 * m
                        copy(whi[r0:r0 + 32, s, m * TA:(m + 1) * TA].bitcast(F32R), eq[r0:r0 + 32, t, :])\
                            .then_inc(ea["hi"], 1)
                    else:
                        r0 = 64 * m
                        copy(wlo[r0:r0 + 64, s, 0:TA].bitcast(F32R), ek[a:a + 64, t, :]).then_inc(ea["hi"], 1)

            act.wait_ge(ea["zeroed"], 4)
            act.wait_ge(rot_done, 8)
            for h in range(2):
                even_hi(h, 0)
                even_hi(h, 1)
            for v in range(4):
                even_exp(v)
            for u, (h, t) in enumerate(units):
                if u + 2 < len(units):
                    even_exp(2 * u + 4)
                    even_exp(2 * u + 5)
                if u:
                    even_copy(u - 1)
                if t >= 4 and h + 2 < A_HEADS:
                    even_hi(h + 2, t - 4)
                if t == 5 and h:
                    even_out(h - 1)
            even_copy(len(units) - 1)
            even_out(A_HEADS - 1)
            for t in range(4):
                if t >= 2:
                    act.wait_ge(ea["sums"], t - 1)
                copy(sq[t % 2], eot[:, t, :], ACT.Square).then_inc(ea["sq"], 1)
            act.wait_ge(ea["sums"], 4)
            tell(copy(hroot[:].rearrange("p t c a -> p t (c a)"),
                      ps[:, 4, 0:64].rearrange("p (t n) -> p t n", n=16)[:, :, 0:12],
                      ACT.Sqrt, bias=eps[:, 0:1], scale=1.0 / 64), ea["root"], 1)

            def out_copy(phase, norm, ctx_too, dst, bias=None):
                for k in range(4):
                    n, s = FIRST[phase] + k, k % 2
                    act.wait_ge(panel_done, n + 1)
                    for j in range(2):
                        kw = dict(bias=par(bias, 2 * k + j)) if bias else {}
                        square(norm, 2 * k + j, ps[:, 2 * s + j, :],
                               ps[:, 4 + s, j * TC:(j + 1) * TC] if ctx_too else None, **kw)
                    if ctx_too:
                        step(copy(dst[:, 2 * k:2 * k + 2, TX:TA],
                                  ps[:, 4 + s, :].rearrange("p (j n) -> p j n", j=2)))
                    if bias:
                        step(copy(dst[:, 2 * k, 0:TX], ps[:, 2 * s, :], bias=par(bias, 2 * k)))
                        last = copy(dst[:, 2 * k + 1, 0:TX], ps[:, 2 * s + 1, :], bias=par(bias, 2 * k + 1))
                    else:
                        last = copy(dst[:, 2 * k:2 * k + 2, 0:TX], ps[:, 2 * s:2 * s + 2, :])
                    last.then_inc(y_free[phase], 1)
                norm_root(norm, ctx_too)

            out_copy("out0", "post0", True, y1)
            pre_norm("pre1", True, "post0")
            hi_parts("pre1", h1hi, 1)

            p0 = FIRST["odd"]
            for k in range(12):
                b, s = k // 2, k % 2
                act.wait_ge(panel_done, p0 + k + 1)
                if b == 2:
                    last = copy(ov[:, :, s * 256:(s + 1) * 256].rearrange("p (b t) n -> p b t n", t=2),
                                ps[:, 3 * s:3 * s + 3, :].rearrange("p b (t n) -> p b t n", t=2))
                else:
                    dst = (oq, ok, None, ogn, oud, ogd)[b][:, 2 * s:2 * s + 2, :]
                    func = ACT.Silu if b in (3, 5) else ACT.Identity
                    if b == 1:
                        step(copy(dst[:, :, TX:TA], ps[:, 4 + s, :].rearrange("p (j n) -> p j n", j=2)))
                    last = copy(dst[:, :, 0:TX], ps[:, 2 * s:2 * s + 2, :], func, scale=0.125 if b == 0 else 1.0)
                tell(last, o_free, k + 1)
            act.wait_ge(panel_done, p0 + 12)
            act.dma_start(dft[:], dram["dft512"]).then_inc(fo["const"], 16)

            def load_bias(h):
                if h:
                    act.wait_ge(oa["bias_in"], 16 * h)
                if h >= 2:
                    act.wait_ge(oa["biased"], 4 * (h - 1))
                act.dma_start(bias_t[h % 2][:], dram["rpb"][h, :, :, :]).then_inc(oa["bias_in"], 16)

            load_bias(0)
            for b in range(8):
                act.wait_ge(fo["half"], 2 * b + 2)
                tell(copy(four[:, b // 2, b % 2 * 512:b % 2 * 512 + 512], ps[:, b % 4, :]), fo["copied"], b + 1)
            act.dma_start(small[:], dram["dist"]).then_inc(dist_in, 16)
            def odd_hi(h):
                a, s, t = h % 2 * 64, h % 2, h // 2
                if h >= 2:
                    act.wait_ge(oa["scores"], 4 * (h - 1))
                copy(whi[a:a + 64, s, 0:TX].bitcast(F32R), oq[a:a + 64, t, :]).then_inc(oa["hi"], 1)
                for r0 in (0, 64):
                    copy(wlo[r0:r0 + 64, s, 0:TA].bitcast(F32R), ok[a:a + 64, t, :]).then_inc(oa["hi"], 1)

            act.wait_ge(oa["zeroed"], 2)
            odd_hi(0)
            odd_hi(1)
            load_bias(1)
            act.wait_ge(fo["out"], 4)

            def odd_exp(u):
                act.wait_ge(oa["negmax"], u + 1)
                if u >= 4:
                    act.wait_ge(oa["transposed"], u - 3)
                scr = ps[:, 2 * (u % 2):2 * (u % 2) + 2, :].rearrange("p b n -> p (b n)")
                act.activation(oprob[u % 4][:, :], scr[:, 0:TA], ACT.Exp, bias=stat[:, 8 + u % 4:9 + u % 4],
                               accum_out=stat[:, 16 + u % 4:17 + u % 4]).then_inc(oa["exp"], 1)

            def odd_copy(u):
                h, t = u // 4, u % 4
                act.wait_ge(oa["transposed"], u + 1)
                if h >= 2:
                    act.wait_ge(oa["pv"], h - 1)
                copy(atx[h % 2][:, :, t * P:(t + 1) * P],
                     ps[:, 4:6, :].rearrange("p b (k n) -> p (b k) n", n=P)[:, 0:6, :]).then_inc(oa["copied"], 1)

            def odd_out(h):
                act.wait_ge(oa["pv"], h + 1)
                tell(copy(oot[h % 2 * 64:h % 2 * 64 + 64, h // 2, :], ps[0:64, 6, :]), oa["out"], h + 1)

            odd_exp(0)
            odd_exp(1)
            for u in range(32):
                h, t = u // 4, u % 4
                if u + 2 < 32:
                    odd_exp(u + 2)
                if t == 2 and h + 2 < 8:
                    load_bias(h + 2)
                if t == 3 and h + 2 < 8:
                    odd_hi(h + 2)
                odd_copy(u)
                if t == 3 and h:
                    odd_out(h - 1)
            odd_out(7)
            out_copy("out1", "post1", False, y1)

            pre_norm("mixpre0", False, "post1")
            hi_parts("mixpre0", h2hi)
            p0 = FIRST["qkv"]
            for k in range(5):
                s = k % 2
                act.wait_ge(panel_done, p0 + k + 1)
                dst = sq8[:, 2 * k:2 * k + 2, :] if k < 4 else sk2[:]
                for j in range(2):
                    ins = copy(dst[:, j, :], ps[:, 2 * s + j, :],
                               bias=bq8[:, 2 * k + j:2 * k + j + 1] if k < 4 else par("b_qkv", 8 + j),
                               scale=0.125 if k < 4 else 1.0)
                    step(ins) if j == 0 else tell(ins, q_free, k + 1)
            for g in range(4):
                for half in range(2):
                    copy(skd[half * 64:half * 64 + 64, g, :],
                         sk2[g % 2 * 64:g % 2 * 64 + 64, g // 2, :]).then_inc(kdup, 1)

            def swa_exp(u):
                k0 = 0 if u % 4 else P
                act.wait_ge(sa["negmax"], u + 1)
                if u >= 4:
                    act.wait_ge(sa["transposed"], u - 3)
                o = 4 * (u % 4)
                for q in range(4):
                    act.activation(
                        sprob[u % 4][:, q, k0:256],
                        ps[:, 2 * (u % 2) + q // 2, q % 2 * 256 + k0:q % 2 * 256 + 256], ACT.Exp,
                        bias=stat[:, 32 + o + q:33 + o + q], accum_out=stat[:, 48 + o + q:49 + o + q])\
                        .then_inc(sa["exp"], 1)
                copy(stat[:, 64 + o:68 + o], stat[:, 64 + o:68 + o], ACT.Exp).then_inc(sa["exp"], 1)

            def swa_copy(u):
                act.wait_ge(sa["transposed"], u + 1)
                if u >= 2:
                    act.wait_ge(sa["pv"], u - 1)
                k0 = 0 if u % 4 else 1
                copy(spt[u % 2][:, k0:2, :], ps[:, 4 + k0:6, :]).then_inc(sa["copied"], 1)

            def swa_out(u):
                g, n = u // 4, u % 4
                act.wait_ge(sa["pv"], u + 1)
                o = ps[0:64, 6 + u % 2, :].rearrange("p (q n) -> p q n", q=4)
                for half in range(2):
                    last = copy(so[half * 64:half * 64 + 64, 2 * g:2 * g + 2, n * P:(n + 1) * P],
                                o[:, 2 * half:2 * half + 2, :])
                    if half:
                        last.then_inc(sa["out"], 1)
                    else:
                        last.then_inc(swa_even, 1)

            def swa_hi(g):
                s = g % 2
                if g >= 2:
                    act.wait_ge(sa["scores"], 4 * (g - 1))
                for half in range(2):
                    r0 = 64 * half
                    copy(whi[r0:r0 + 64, s, half * 1024:half * 1024 + 1024].bitcast(F32R)
                         .rearrange("p (j n) -> p j n", j=2), sq8[r0:r0 + 64, 2 * g:2 * g + 2, :]).then_inc(sa["hi"], 1)
                copy(wlo[:, s, 0:TX].bitcast(F32R), skd[:, g, :]).then_inc(sa["hi"], 1)

            act.wait_ge(panel_done, FIRST["qkv"] + 6)
            act.wait_ge(kdup, 8)
            swa_hi(0)
            swa_hi(1)
            swa_exp(0)
            swa_exp(1)
            for u in range(16):
                n = u % 4
                if u + 2 < 16:
                    swa_exp(u + 2)
                if n == 3 and u < 8:
                    swa_hi(u // 4 + 2)
                swa_copy(u)
                if u:
                    swa_out(u - 1)
            swa_out(15)
            out_copy("wo", "mixpost0", False, ywo, "b_o")

            def ffn(layer):
                f = ff[layer]
                p0 = FIRST[f"ffn{layer}_in"]
                c0 = layer * FT
                pre_norm(f"ffnpre{layer}", False, f"mixpost{layer}")
                hi_parts(f"ffnpre{layer}", h2hi)

                def panel(n, s, first):
                    act.wait_ge(panel_done, p0 + n + 1)
                    if not first:
                        act.wait_ge(f["gelu"], n - 1)
                    tell(copy(tap[s], ps[:, 2 * s, :], scale=par("cw2", c0 + n), bias=par("cb", c0 + n)),
                                 f["tap"], n + 1)
                    act.wait_ge(f["taps"], n + 1)
                    if not first:
                        act.wait_ge(f["gated"], n - 1)
                    tell(copy(gel[s], tap[s], ACT.Gelu_apprx_tanh), f["gelu"], n + 1)
                act.preload_act_table(ACT.Gelu_apprx_tanh)
                for s in range(2):
                    panel(s, s, True)
                with act.Fori(1, 11) as i:
                    for s in range(2):
                        panel(2 * i + s, s, False)
                long_copy(f"ffn{layer}_out", f"ffnpost{layer}")

            def long_copy(phase, norm):
                p0 = FIRST[phase]

                def pair(i, first):
                    for j in range(2):
                        act.wait_ge(panel_done, p0 + 4 * i + 2 * j + 2)
                        if not first:
                            act.wait_ge(n_acc, (KT + 1) * NORM[norm] + 2 * i + j)
                        copy(sq[j][:, 0:TX], ps[:, j, :], ACT.Square).then_inc(n_sq, 1)
                        copy(y2[:, ds(2 * i + j, 1), :], ps[:, j:j + 1, :]).then_inc(y_free[phase], 1)
                act.preload_act_table(ACT.Identity)
                pair(0, True)
                with act.Fori(1, 4) as i:
                    pair(i, False)
                norm_root(norm, False)

            ffn(0)
            pre_norm("mixpre1", False, "ffnpost0")
            hi_parts("mixpre1", h2hi)
            act.preload_act_table(ACT.Gelu_apprx_tanh)
            with act.Fori(0, 6) as i:
                for s in range(2):
                    act.wait_ge(panel_done, FIRST["sgu_v"] + 2 * i + s + 1)
                    for b in range(2):
                        copy(vtok[:, ds(4 * i + 2 * s, 2), 2 * b:2 * b + 2, :].rearrange("p d c n -> p c d n"),
                             ps[:, 2 * s + b, :].rearrange("p (c d n) -> p c d n", c=2, d=2),
                             ACT.Gelu_apprx_tanh).then_inc(sg["v"], 1)
            for b in range(2):
                act.wait_ge(sg["rowsum"], 1)
                copy(wave[:, b, :], ps[:, 4 + b, :]).then_inc(sg["rows_copied"], 1)
            act.wait_ge(sg["moments"], 4)
            tell(copy(stat[:, 8:12], stat[:, 4:8], ACT.Sqrt, bias=eps[:, 0:1]), sg["root"], 1)
            for k in range(12):
                s = k % 2
                act.wait_ge(panel_done, FIRST["sgu_u"] + k + 1)
                if k >= 2:
                    act.wait_ge(sg["gated"], 2 * (k - 1))
                tell(copy(ug[s], ps[:, 2 * s:2 * s + 2, :], ACT.Gelu_apprx_tanh), sg["gelu"], k + 1)
            long_copy("sgu_out", "mixpost1")
            ffn(1)

        @block.vector
        def _(dve):
            order = [0, 0]

            def step(ins):
                order[1] += 1
                ins.then_inc(dve_order, 1)
                dve.wait_ge(dve_order, order[0] + order[1])

            def tell(ins, done, value):
                ins.then_inc(done, 1)
                dve.wait_ge(done, value)

            def loop(first, last, steps, body):
                base = order[0] + order[1]
                with dve.Fori(first, last) as i:
                    order[:] = [base + i * steps - first * steps, 0]
                    body(i)
                    assert order[1] == steps
                order[:] = [base + (last - first) * steps, 0]

            def split_panel(n, slot, width, load_count):
                dve.wait_ge(raw_loaded[slot], load_count)
                if not isinstance(n, int) or n >= 2:
                    dve.wait_ge(panel_done, n - 1)
                step(dve.tensor_copy(whi[:, slot, 0:width].bitcast(F32R), raw[:, slot, 0:width]))
                tell(dve.tensor_tensor(wlo[:, slot, 0:width].bitcast(F32R), raw[:, slot, 0:width], whi[:, slot, 0:width],
                                               ALU.subtract), split_done, n + 1)

            def split_at(n):
                if n < N_PANELS:
                    split_panel(n, n % 2, WIDTH_OF[n], 16 * (n // 2 + 1))

            def splits(phase, a, b, last=True):
                p0 = FIRST[phase]
                width = dict((k, w) for k, _, w in PHASES)[phase]
                if b - a > 2:
                    def body(i):
                        split_panel(p0 + 2 * i + 1, 1, width, 16 * (p0 // 2 + i + 1))
                        split_panel(p0 + 2 * i + 2, 0, width, 16 * (p0 // 2 + i + 2))
                    loop(a // 2, b // 2 - 1, 2, body)
                split_at(p0 + b - 1)
                if last:
                    split_at(p0 + b)

            def split_tensor(hi, lo, at, full, done=None, value=None):
                step(dve.tensor_copy(hi[at], full))
                ins = dve.tensor_tensor(lo[at], full, hi[at].bitcast(F32), ALU.subtract)
                tell(ins, done, value) if done is not None else step(ins)

            def norm_inverse(key):
                dve.wait_ge(n_rt, 2 * NORM[key] + 1)
                tell(dve.reciprocal(root[:], root[:]), n_rt, 2 * NORM[key] + 2)

            def pre_norm(key, ctx_too, hi, lo, mul, shift=None):
                dve.wait_ge(n_mm, 2 * NORM[key] + 2)
                per = 2 if ctx_too else 1

                def low(kt):
                    full = sq[kt % 2]
                    dve.wait_ge(n_hi[key], per * (kt + 1))
                    if ctx_too:
                        step(dve.scalar_tensor_tensor(out=lo[:, kt, TX:TA], in0=full[:, TX:TA], scalar=shift(kt, 1),
                                                      in1=hi[:, kt, TX:TA].bitcast(F32), op0=ALU.add, op1=ALU.subtract))
                        dve.scalar_tensor_tensor(out=lo[:, kt, 0:TX], in0=full[:, 0:TX], scalar=shift(kt, 0),
                                                 in1=hi[:, kt, 0:TX].bitcast(F32), op0=ALU.add, op1=ALU.subtract)\
                            .then_inc(n_ok[key], 1)
                    else:
                        dve.tensor_tensor(lo[:, kt, :], full[:, 0:TX], hi[:, kt, :].bitcast(F32), ALU.subtract)\
                            .then_inc(n_ok[key], 1)

                for kt in range(KT):
                    full = sq[kt % 2]
                    if kt >= 2:
                        dve.wait_ge(n_ok[key], kt - 1)
                    if ctx_too:
                        dve.scalar_tensor_tensor(out=full[:, TX:TA], in0=cx[:, kt, :], scalar=mul(kt, 1), in1=rc,
                                                 op0=ALU.mult, op1=ALU.mult).then_inc(n_full[key], 1)
                    dve.scalar_tensor_tensor(out=full[:, 0:TX], in0=x[:, kt, :], scalar=mul(kt, 0), in1=rx,
                                             op0=ALU.mult, op1=ALU.mult).then_inc(n_full[key], 1)
                    if kt:
                        low(kt - 1)
                low(KT - 1)
                dve.wait_ge(n_ok[key], KT)

            def post_norm(key, y, copied, ctx_too, mul):
                norm_inverse(key)
                dve.wait_ge(y_free[copied], 4 if y is not y2 else KT)
                dve.wait_ge(n_mm, 2 * NORM[key] + 2)
                per = 2 if ctx_too else 1

                def add(kt):
                    dve.wait_ge(n_full[key], per * (kt + 1))
                    if ctx_too:
                        step(dve.tensor_tensor(cx[:, kt, :], cx[:, kt, :], y[:, kt, TX:TA], ALU.add))
                    dve.tensor_tensor(x[:, kt, :], x[:, kt, :], y[:, kt, 0:TX], ALU.add).then_inc(n_ok[key], 1)

                for kt in range(KT):
                    for c in range(per):
                        yy = y[:, kt, TX:TA] if c else y[:, kt, 0:TX]
                        dve.scalar_tensor_tensor(out=yy, in0=yy, scalar=mul(kt, c), in1=rc if c else rx,
                                                 op0=ALU.mult, op1=ALU.mult).then_inc(n_full[key], 1)
                    if kt:
                        add(kt - 1)
                add(KT - 1)
                dve.wait_ge(n_ok[key], KT)

            step(dve.memset(eps[:], EPS))
            dve.wait_ge(params_in, 32)
            dve.memset(lam_t[:], 0.0).then_inc(cond_ready, 1)
            step(dve.tensor_scalar(subl[:], par("subln", 0), 1.0 - LAM0, None, ALU.mult))
            step(dve.tensor_scalar(bq8[:], par("b_qkv", 0, 8), 0.125, None, ALU.mult))
            dve.wait_ge(cond_ready, 1)
            norm_inverse("pre0")
            split_at(0)

            def modulation(layer, a, b, count):
                cols = ps[:, 6, 64 * layer:64 * layer + 48].rearrange("p (k c) -> p k c", c=2)
                for c in range(2):
                    tell(dve.tensor_tensor(modc[layer][:, a:b, c], cols[:, a:b, c],
                                           par("b_mod", 24 * layer + a, b - a), ALU.add), mod_ready, count + c)

            def input_scale(layer):
                for c in range(2):
                    step(dve.scalar_tensor_tensor(out=amul[:, :, c], in0=modc[layer][:, 8:16, c], scalar=1.0,
                                                  in1=par("pre", 8 * layer, 8), op0=ALU.add, op1=ALU.mult))

            def output_scale(layer):
                for c in range(2):
                    step(dve.tensor_tensor(gmul[:, :, c], modc[layer][:, 16:24, c], par("post", 8 * layer, 8), ALU.mult))

            dve.wait_ge(mod_cols, 8)
            modulation(0, 0, 16, 1)
            input_scale(0)
            pre_norm("pre0", True, h1hi, h1lo, lambda kt, c: amul[:, kt, c:c + 1],
                     lambda kt, c: modc[0][:, kt, c:c + 1])
            for n in range(1, 4):
                split_at(n)
            dve.wait_ge(mod_cols, 12)
            modulation(0, 16, 24, 3)
            output_scale(0)
            for n in range(4, 9):
                split_at(n)
            step(dve.memset(zpad[:, 0:771], 0.0))
            for j in range(4):
                split_at(9 + 2 * j)
                dve.wait_ge(cb_in, j + 1)
                step(dve.tensor_tensor(zpad[:, 514:770], eob[:, j, TX:TA], ps[:, 4, TC:2 * TC], ALU.mult))
                tell(dve.tensor_tensor(zpad[:, 1:513], eob[:, j, 0:TX], ps[:, 1, :], ALU.mult), zed, j + 1)
                if j < 3:
                    split_at(10 + 2 * j)
                cw = [par("conv_b", 4 * tap_i + j) for tap_i in range(3)]
                step(dve.tensor_scalar(ycv[:, 0:769], zpad[:, 1:770], cw[1], None, ALU.mult))
                for a in (0, 2):
                    step(dve.scalar_tensor_tensor(out=ycv[:, 0:769], in0=zpad[:, a:a + 769], scalar=cw[a],
                                                  in1=ycv[:, 0:769], op0=ALU.mult, op1=ALU.add))
                dve.wait_ge(sg_in, j + 1)
                step(dve.tensor_tensor(sgb[:, TX:TA], sgb[:, TX:TA], ps[:, 5, 0:TC], ALU.mult))
                step(dve.tensor_tensor(sgb[:, 0:TX], sgb[:, 0:TX], ps[:, 2, :], ALU.mult))
                step(dve.tensor_tensor(eob[:, j, TX:TA], sgb[:, TX:TA], ycv[:, 513:769], ALU.mult))
                tell(dve.tensor_tensor(eob[:, j, 0:TX], sgb[:, 0:TX], ycv[:, 0:512], ALU.mult), b_free, j + 1)
            dve.wait_ge(mod_cols, 24)
            modulation(1, 0, 24, 5)
            dve.wait_ge(panel_done, 16)
            step(dve.memset(sq[0], 0.0))
            for s in range(2):
                dve.tensor_copy(whi[:, s, 0:2 * TA].bitcast(F32R).rearrange("p (m n) -> p m n", m=2),
                                sq[0].unsqueeze(1).broadcast_to([P, 2, TA])).then_inc(ea["zeroed"], 1)
                other = 64 - 64 * s
                dve.tensor_copy(wlo[other:other + 64, s, TA:2 * TA].bitcast(F32R), sq[0][other:other + 64, :])\
                    .then_inc(ea["zeroed"], 1)
            dve.wait_ge(consts_in, 48)
            for t in range(8):
                src = (eq, ek)[t // 4][:, t % 4, 0:TX]
                dve.wait_ge(rot_mm, t + 1)
                tmp = sgb[:, 0:TX]
                step(dve.tensor_tensor(tmp, ps[:, t % 2, :], wave[:, 1, :], ALU.mult))
                step(dve.tensor_tensor(src, src, wave[:, 0, :], ALU.mult))
                tell(dve.tensor_tensor(src, src, tmp, ALU.add), rot_done, t + 1)
            lamp = par("lam", 0, 128).rearrange("p (a b n) -> p a b n", a=2, b=2)
            step(dve.tensor_tensor(lam_t[:].rearrange("p (a n) -> p a n", a=2), lamp[:, :, 0, :], lamp[:, :, 1, :], ALU.mult))
            tell(dve.tensor_reduce(lam4[:, 0:2], lam_t[:].rearrange("p (a n) -> p a n", a=2), AX, ALU.add), ea["lam"], 1)
            dve.wait_ge(ea["lam_exp"], 1)
            step(dve.tensor_tensor(lam4[:, 2:3], lam4[:, 1:2], lam4[:, 0:1], ALU.subtract))
            step(dve.tensor_scalar(lam4[:, 3:4], lam4[:, 2:3], -LAM0, None, ALU.add))

            units = [(h, t) for h in range(A_HEADS) for t in range(6)]

            def even_max(v):
                n = TA if units[v // 2][1] < 4 else TC
                dve.wait_ge(ea["scores"], v + 1)
                scr = ps[:, 2 * (v % 2):2 * (v % 2) + 2, :].rearrange("p b n -> p (b n)")
                dve.tensor_reduce(stat[:, v % 8:v % 8 + 1], scr[:, 0:n], AX, ALU.max, negate=True)\
                    .then_inc(ea["negmax"], 1)

            for v in range(4):
                even_max(v)
            for u, (h, t) in enumerate(units):
                if u + 2 < len(units):
                    even_max(2 * u + 4)
                    even_max(2 * u + 5)
                n = TA if t < 4 else TC
                o = 2 * (u % 4)
                dve.wait_ge(ea["exp"], 2 * u + 2)
                step(dve.reciprocal(stat[:, 16 + o:18 + o], stat[:, 8 + o:10 + o]))
                step(dve.tensor_tensor(stat[:, 17 + o:18 + o], stat[:, 17 + o:18 + o], lam4[:, 3:4], ALU.mult))
                p = prob[u % 4]
                step(dve.tensor_scalar(p[:, 0, 0:n], p[:, 0, 0:n], stat[:, 16 + o:17 + o], None, ALU.mult))
                tell(dve.scalar_tensor_tensor(out=p[:, 0, 0:n], in0=p[:, 1, 0:n], scalar=stat[:, 17 + o:18 + o],
                                              in1=p[:, 0, 0:n], op0=ALU.mult, op1=ALU.add), ea["probs"], u + 1)
                if (h, t) == (7, 1):
                    dve.wait_ge(ea["scores"], 84)
                    split_at(FIRST["out0"])
            dve.wait_ge(ea["out"], 8)
            for t in range(4):
                step(dve.scalar_tensor_tensor(out=ega[:, t, :], in0=eot[:, t, :], scalar=subl[:, 0:1], in1=ega[:, t, :],
                                              op0=ALU.mult, op1=ALU.mult))
            for t in range(2):
                split_tensor(h1hi, h1lo, np.s_[:, 4 + t, :], eob[:, t, :], ea["mixed"], t + 1)
            dve.wait_ge(ea["root"], 1)
            step(dve.reciprocal(hroot[:], hroot[:]))
            for t in range(4):
                dve.tensor_copy(hwide[:, t, :, :].rearrange("p c (a n) -> p c a n", a=2),
                                hroot[:, t, :, :].unsqueeze(3).broadcast_to([P, 6, 2, 64])).then_inc(ea["inverse"], 1)
            for t in range(2, 4):
                split_tensor(h1hi, h1lo, np.s_[:, 4 + t, :], eob[:, t, :], ea["mixed"], t + 1)
            for t in range(4):
                dve.wait_ge(ea["spread"], t + 1)
                b = (6, 2)[t % 2]
                tell(dve.tensor_tensor(ega[:, t, :], ega[:, t, :],
                                       ps[:, b:b + 2, :].rearrange("p b n -> p (b n)")[:, 0:TA], ALU.mult),
                     ea["normed"], t + 1)
                split_tensor(h1hi, h1lo, np.s_[:, t, :], ega[:, t, :], ea["mixed"], t + 5)
            splits("out0", 0, 4)
            post_norm("post0", y1, "out0", True, lambda kt, c: gmul[:, kt, c:c + 1])
            input_scale(1)
            output_scale(1)
            norm_inverse("pre1")
            pre_norm("pre1", True, h1hi, h1lo, lambda kt, c: amul[:, kt, c:c + 1],
                     lambda kt, c: modc[1][:, kt, c:c + 1])
            splits("odd", 0, 12, last=False)
            dve.wait_ge(panel_done, FIRST["odd"] + 12)
            step(dve.memset(sq[0], 0.0))
            for s in range(2):
                other = 64 - 64 * s
                dve.tensor_copy(wlo[other:other + 64, s, TA:2 * TA].bitcast(F32R), sq[0][other:other + 64, :])\
                    .then_inc(oa["zeroed"], 1)
            for f in range(4):
                dve.wait_ge(fo["full"], f + 1)
                tell(dve.tensor_tensor(ogd[:, f, :], ogd[:, f, :], ps[:, 4 + f, :], ALU.mult), fo["out"], f + 1)

            def odd_max(u):
                h, t = u // 4, u % 4
                dve.wait_ge(oa["scores"], u + 1)
                if t == 0:
                    dve.wait_ge(oa["bias"], h + 1)
                b = 2 * (u % 2)
                bt = bias_t[h % 2][:, 7 - 2 * t:15 - 2 * t, :].rearrange("p r n -> p (r n)")
                tell(dve.tensor_tensor(ps[:, b, :], ps[:, b, :], bt, ALU.add), oa["biased"], u + 1)
                scr = ps[:, b:b + 2, :].rearrange("p b n -> p (b n)")
                tell(dve.tensor_reduce(stat[:, 8 + u % 4:9 + u % 4], scr[:, 0:TA], AX, ALU.max, negate=True),
                       oa["negmax"], u + 1)

            odd_max(0)
            odd_max(1)
            for u in range(32):
                if u + 2 < 32:
                    odd_max(u + 2)
                dve.wait_ge(oa["exp"], u + 1)
                step(dve.reciprocal(stat[:, 24 + u % 4:25 + u % 4], stat[:, 16 + u % 4:17 + u % 4]))
                dve.tensor_scalar(oprob[u % 4][:, :], oprob[u % 4][:, :], stat[:, 24 + u % 4:25 + u % 4], None, ALU.mult)\
                    .then_inc(oa["probs"], 1)
                if u == 28:
                    split_at(FIRST["out1"])
            dve.wait_ge(oa["out"], 8)
            for t in range(4):
                split_tensor(o1hi, o1lo, np.s_[:, 4 + t, :], ogd[:, t, :], oa["mixed"], t + 1)
            for t in range(4):
                step(dve.tensor_tensor(oot[:, t, :], oot[:, t, :], ogn[:, t, :], ALU.mult))
                split_tensor(o1hi, o1lo, np.s_[:, t, :], oot[:, t, :], oa["mixed"], t + 5)
            splits("out1", 0, 4)
            post_norm("post1", y1, "out1", False, lambda kt, c: gmul[:, kt, c:c + 1])

            norm_inverse("mixpre0")
            pre_norm("mixpre0", False, h2hi, h2lo, lambda kt, c: par("mix_pre", kt))
            splits("qkv", 0, 6, last=False)
            dve.wait_ge(panel_done, FIRST["qkv"] + 6)
            tell(dve.tensor_tensor(sv[:], ps[:, 6:8, :].rearrange("p b (t n) -> p (b t) n", t=2),
                                     par("b_v", 0, 256).unsqueeze(1).broadcast_to([P, 4, 256]), ALU.add), v_free, 1)
            dve.wait_ge(alibi_ready, N_HEADS)

            def swa_max(u):
                g, n = u // 4, u % 4
                k0 = 0 if n else P
                o = 4 * (u % 4)
                dve.wait_ge(sa["scores"], u + 1)
                scr = ps[:, 2 * (u % 2):2 * (u % 2) + 2, :].rearrange("p b (q n) -> p (b q) n", q=2)[:, :, k0:256]
                step(dve.tensor_tensor(scr, scr, alibi[:, 4 * g:4 * g + 4, k0:256], ALU.add))
                step(dve.tensor_reduce(stat[:, o:o + 4], scr, AX, ALU.max))
                step(dve.tensor_tensor(stat[:, o:o + 4], stat[:, o:o + 4], par("sinks", 4 * g, 4), ALU.max))
                step(dve.tensor_tensor(stat[:, 64 + o:68 + o], par("sinks", 4 * g, 4), stat[:, o:o + 4], ALU.subtract))
                tell(dve.tensor_scalar(stat[:, 32 + o:36 + o], stat[:, o:o + 4], -1.0, None, ALU.mult),
                       sa["negmax"], u + 1)

            def swa_split(g):
                dve.wait_ge(sa["out"], 4 * (g + 1))
                dve.wait_ge(swa_even, 4 * (g + 1))
                for t in range(2 * g, 2 * g + 2):
                    split_tensor(h2hi, h2lo, np.s_[:, t, :], so[:, t, :], sa["mixed"], t + 1)

            swa_max(0)
            swa_max(1)
            for u in range(16):
                if u + 2 < 16:
                    swa_max(u + 2)
                k0 = 0 if u % 4 else P
                o = 4 * (u % 4)
                dve.wait_ge(sa["exp"], 5 * (u + 1))
                step(dve.tensor_tensor(stat[:, 80 + o:84 + o], stat[:, 48 + o:52 + o], stat[:, 64 + o:68 + o], ALU.add))
                step(dve.reciprocal(stat[:, 80 + o:84 + o], stat[:, 80 + o:84 + o]))
                p = sprob[u % 4][:, :, k0:256]
                tell(dve.tensor_tensor(p, p, stat[:, 80 + o:84 + o].unsqueeze(2).broadcast_to([P, 4, 256 - k0]),
                                         ALU.mult), sa["probs"], u + 1)
                if u % 4 == 2 and u > 4:
                    swa_split(u // 4 - 1)
                if u == 12:
                    split_at(FIRST["wo"])
            swa_split(3)
            splits("wo", 0, 4)
            post_norm("mixpost0", ywo, "wo", False, lambda kt, c: par("mix_post", kt))

            def ffn(layer):
                f = ff[layer]
                p0 = FIRST[f"ffn{layer}_in"]
                c0 = layer * FT
                norm_inverse(f"ffnpre{layer}")
                pre_norm(f"ffnpre{layer}", False, h2hi, h2lo, lambda kt, c: par("ffn_pre", 8 * layer + kt))

                def taps(n, s):
                    dve.wait_ge(f["tap"], n + 1)
                    step(dve.scalar_tensor_tensor(out=tap[s][:, 1:512], in0=ps[:, 2 * s, 0:511],
                                                        scalar=par("cw1", c0 + n), in1=tap[s][:, 1:512],
                                                        op0=ALU.mult, op1=ALU.add))
                    tell(dve.scalar_tensor_tensor(out=tap[s][:, 2:512], in0=ps[:, 2 * s, 0:510],
                                                          scalar=par("cw0", c0 + n), in1=tap[s][:, 2:512],
                                                          op0=ALU.mult, op1=ALU.add), f["taps"], n + 1)

                def gate(n, s):
                    dve.wait_ge(f["gelu"], n + 1)
                    step(dve.tensor_tensor(gel[s], gel[s], ps[:, 2 * s + 1, :], ALU.mult))
                    split_tensor(mhi, mlo, np.s_[:, ds(n, 1), :], gel[s].unsqueeze(1), f["gated"], n + 1)

                split_at(p0 + 1)
                taps(0, 0)
                split_at(p0 + 2)
                gate(0, 0)
                taps(1, 1)

                def body(i):
                    split_panel(p0 + 2 * i + 1, 1, 2048, 16 * (p0 // 2 + i + 1))
                    gate(2 * i - 1, 1)
                    taps(2 * i, 0)
                    split_panel(p0 + 2 * i + 2, 0, 2048, 16 * (p0 // 2 + i + 2))
                    gate(2 * i, 0)
                    taps(2 * i + 1, 1)
                loop(1, 10, 8, body)
                split_at(p0 + 21)
                gate(19, 1)
                taps(20, 0)
                split_at(p0 + 22)
                gate(20, 0)
                taps(21, 1)
                gate(21, 1)
                splits(f"ffn{layer}_out", 0, 16)
                post_norm(f"ffnpost{layer}", y2, f"ffn{layer}_out", False, lambda kt, c: par("ffn_post", 8 * layer + kt))

            ffn(0)
            norm_inverse("mixpre1")
            pre_norm("mixpre1", False, h2hi, h2lo, lambda kt, c: par("mix_pre", 8 + kt))
            p0 = FIRST["sgu_v"]

            def v_stats(i):
                dve.wait_ge(sg["v"], 4 * (i + 1))
                for c in range(4):
                    step(dve.bn_stats(bns[:, c, ds(i, 1), :].rearrange("p a n -> p (a n)"),
                                            vtok[:, ds(4 * i, 4), c, :]))

            def v_body(i):
                split_panel(p0 + 2 * i + 1, 1, 2048, 16 * (p0 // 2 + i + 1))
                split_panel(p0 + 2 * i + 2, 0, 2048, 16 * (p0 // 2 + i + 2))
                v_stats(i)
            loop(0, 6, 6, v_body)
            for c in range(4):
                step(dve.bn_aggr(stat[:, 16 + 2 * c:18 + 2 * c], bns[:, c, :, :]))
                tell(dve.tensor_copy(stat[:, 4 + c:5 + c], stat[:, 17 + 2 * c:18 + 2 * c]), sg["moments"], c + 1)
            dve.wait_ge(sg["root"], 1)
            step(dve.reciprocal(stat[:, 12:16], stat[:, 8:12]))
            for c in range(4):
                tell(dve.tensor_scalar(vtok[:, :, c, :], vtok[:, :, c, :], stat[:, 16 + 2 * c:17 + 2 * c],
                                         stat[:, 12 + c:13 + c], ALU.subtract, ALU.mult), sg["normed"], c + 1)
            dve.wait_ge(sg["rows_copied"], 2)
            dve.wait_ge(late_in, 32)
            p0 = FIRST["sgu_u"]
            for k in range(12):
                s = k % 2
                split_at(p0 + k + 1)
                for j in range(2):
                    dt = 2 * k + j
                    g = dt // 3
                    base = small[:, 0:P]
                    step(dve.scalar_tensor_tensor(out=base, in0=wave[:, g // 4, g % 4 * P:g % 4 * P + P],
                                                  scalar=par("ln_b", dt), in1=bsb[:, g, :], op0=ALU.mult, op1=ALU.add))
                    if j == 0:
                        dve.wait_ge(sg["uhalf"], k + 1)
                        dve.wait_ge(sg["gelu"], k + 1)
                    mixed = ps[:, 4 + 2 * s + j, :].rearrange("p (c n) -> p c n", c=4)
                    step(dve.scalar_tensor_tensor(out=mixed, in0=mixed, scalar=par("ln_g", dt),
                                                  in1=base.unsqueeze(1).broadcast_to([P, 4, P]),
                                                  op0=ALU.mult, op1=ALU.add))
                    step(dve.tensor_tensor(ug[s][:, j, :], ug[s][:, j, :], ps[:, 4 + 2 * s + j, :], ALU.mult))
                    split_tensor(mhi, mlo, np.s_[:, dt, :], ug[s][:, j, :], sg["gated"], dt + 1)
            splits("sgu_out", 0, 16)
            post_norm("mixpost1", y2, "sgu_out", False, lambda kt, c: par("mix_post", 8 + kt))
            ffn(1)

        @block.gpsimd
        def _(pool):
            def add_squares(i):
                key = NORMS[i]
                n = TA if key in ("pre0", "post0", "pre1") else TX
                if i:
                    pool.wait_ge(n_mm, 2 * NORM[NORMS[i - 1]] + 1)
                pool.memset(acc[:, 0:n], 0.0).then_inc(n_acc, 1)
                for kt in range(KT):
                    pool.wait_ge(n_sq, KT * NORM[key] + kt + 1)
                    pool.wait_ge(n_acc, (KT + 1) * NORM[key] + kt + 1)
                    pool.tensor_tensor(acc[:, 0:n], acc[:, 0:n], sq[kt % 2][:, 0:n], ALU.add).then_inc(n_acc, 1)

            add_squares(0)
            pool.wait_ge(late_in, 32)
            pool.affine_select(out=wst[:], in_=wst[:], compare_op=ALU.is_ge, fill=0.0, base=0,
                               pattern=[[0, SG_GROUPS], [1, P]], channel_multiplier=-1).then_inc(sg["ws"], 1)

            def lo_part(done, count, hi, full, out):
                pool.tensor_tensor(out.bitcast(F32R), full, hi, ALU.subtract).then_inc(done, 1)
                pool.wait_ge(done, count)

            pool.wait_ge(sg["ws"], 1)

            for h in range(A_HEADS):
                a, s, t = h % 2 * 64, h % 2, h // 2
                pool.wait_ge(ea["hi"], 4 * (h + 1))
                for m in range(2):
                    r0, r1 = a + 32 * m, 64 - a + 32 * m
                    lo_part(ea["lo"], 3 * h + m + 1, whi[r0:r0 + 32, s, m * TA:(m + 1) * TA], eq[r0:r0 + 32, t, :],
                            whi[r1:r1 + 32, s, m * TA:(m + 1) * TA])
                lo_part(ea["lo"], 3 * h + 3, wlo[a:a + 64, s, 0:TA], ek[a:a + 64, t, :], wlo[a:a + 64, s, TA:2 * TA])
            add_squares(1)
            add_squares(2)
            pool.wait_ge(consts_in, 48)
            for h in range(8):
                pool.wait_ge(oa["bias_in"], 16 * (h + 1))
                v = bias_t[h % 2][:]
                pool.tensor_tensor(v, v, mask64[:].unsqueeze(1).broadcast_to([P, 15, 64]), ALU.add)\
                    .then_inc(oa["bias"], 1)
                pool.wait_ge(oa["bias"], h + 1)
                a, s, t = h % 2 * 64, h % 2, h // 2
                pool.wait_ge(oa["hi"], 3 * (h + 1))
                lo_part(oa["lo"], 2 * h + 1, whi[a:a + 64, s, 0:TX], oq[a:a + 64, t, :], whi[64 - a:128 - a, s, 0:TX])
                lo_part(oa["lo"], 2 * h + 2, wlo[a:a + 64, s, 0:TA], ok[a:a + 64, t, :], wlo[a:a + 64, s, TA:2 * TA])
            add_squares(3)
            add_squares(4)
            pool.wait_ge(n_ok["mixpre0"], KT)
            pool.wait_ge(dist_in, 16)
            for n in range(N_HEADS):
                slope = 2.0 ** (-8.0 * (n // 4 * 4 + SWA_ORDER[n % 4] + 1) / N_HEADS)
                pool.tensor_scalar(alibi[:, n, :], small[:, :], -slope, None, ALU.mult).then_inc(alibi_ready, 1)
            pool.wait_ge(alibi_ready, N_HEADS)
            for g in range(KV_HEADS):
                s = g % 2
                pool.wait_ge(sa["hi"], 3 * (g + 1))
                for half in range(2):
                    r0, r1, cols = 64 * half, 64 - 64 * half, slice(half * 1024, half * 1024 + 1024)
                    lo_part(sa["lo"], 3 * g + half + 1, whi[r0:r0 + 64, s, cols], sq8[r0:r0 + 64, 2 * g:2 * g + 2, :]
                            .rearrange("p j n -> p (j n)"), whi[r1:r1 + 64, s, cols])
                lo_part(sa["lo"], 3 * g + 3, wlo[:, s, 0:TX], skd[:, g, :], wlo[:, s, TX:2 * TX])
            add_squares(5)
            add_squares(6)
            pool.wait_ge(ff[0]["gated"], FT)
            add_squares(7)
            add_squares(8)
            pool.wait_ge(sg["gated"], ST)
            add_squares(9)
            add_squares(10)
            pool.wait_ge(ff[1]["gated"], FT)
            add_squares(11)


def _constants():
    f = np.float32
    eye = np.eye(P, dtype=f)
    blk = np.zeros((P, P), f)
    blk[:64, :64] = blk[64:, 64:] = 1
    rot = np.zeros((P, P), f)
    for m in range(P):
        rot[m ^ 8, m] = -1.0 if m % 16 < 8 else 1.0
    mats = np.stack([eye, np.ones((P, P), f), blk, rot], 1)
    t = np.arange(TX)
    inv = (np.float32(10000.0) ** (-np.arange(8, dtype=f) / f(8))).astype(f)
    ang = np.zeros((P, TX), f)
    for m in range(P):
        pos = t // 64 if m % 32 < 16 else t % 64
        ang[m] = pos.astype(f) * inv[m % 8]
    wave = np.stack([np.cos(ang.astype(np.float64)), np.sin(ang.astype(np.float64))], 1).astype(f)
    k = np.arange(64)
    a = 2 * np.pi * (np.outer(k, k) % 64) / 64
    dft64 = np.zeros((P, 2, P), f)
    for g in range(2):
        dft64[64 * g:64 * g + 64, 0, 64 * g:64 * g + 64] = np.cos(a)
        dft64[64 * g:64 * g + 64, 1, 64 * g:64 * g + 64] = -np.sin(a)
    n = np.arange(TX)
    b = 2 * np.pi * (np.outer(n, n) % TX) / TX
    scale = 1 / math.sqrt(TX * 64)
    dft512 = np.stack([np.cos(b) * scale, np.sin(b) * scale]).astype(f)
    dft512 = dft512.reshape(2, 4, P, TX).transpose(2, 0, 1, 3)
    c = np.arange(64)
    start = np.clip(c - 8, 0, 48)
    outside = (c[None] < start[:, None]) | (c[None] >= start[:, None] + 16)
    mask64 = np.tile(np.where(outside, f(MASKED), f(0)), (2, 1)).astype(f)
    dist = np.arange(P)[:, None] + P - np.arange(256)[None]
    dist = np.where((dist >= 0) & (dist < P), dist, 1e33).astype(f)
    return dict(mats=mats, wave=wave, dft64=dft64.reshape(P, 256), dft512=dft512, mask64=mask64,
                dist=dist)


def _columns(v):
    return np.asarray(v).reshape(-1, P).T


def _every(v):
    v = np.asarray(v).reshape(1, -1)
    return np.broadcast_to(v, (P, v.shape[1]))


def _panels(w, cols=256):
    k, n = w.shape
    return w.reshape(k // P, P, n // cols, cols).transpose(2, 1, 0, 3).reshape(n // cols, P, -1)


def _half_panels(w):
    k, n = w.shape
    return w.reshape(2, k // 2 // P, P, n // P, P).transpose(3, 0, 2, 1, 4).reshape(2 * n // P, P, -1)


def _interleaved(*ws):
    k, n = ws[0].shape
    w = np.stack([m.reshape(k, n // P, P) for m in ws], 2).reshape(k, -1)
    return _panels(w)


def _alternate(a, b):
    return np.stack([a, b], 1).reshape(-1, *a.shape[1:])


def kernel(**inputs):
    import concourse.bacc as bacc
    from concourse.bass_utils import run_bass_kernel_spmd

    g = {k: np.asarray(v) for k, v in inputs.items()}
    params = dict(
        b_mod=_columns(g["b_mod"]), pre=_columns(g["norm_pre"]), post=_columns(g["norm_post"]),
        conv_b=_columns(g["conv_b"]), subln=_columns(np.tile(g["subln_a"][0], 2)),
        mix_pre=_columns(g["norm_mix_pre_2"]), mix_post=_columns(g["norm_mix_post_2"]),
        ffn_pre=_columns(g["norm_ffn_pre_2"]), ffn_post=_columns(g["norm_ffn_post_2"]),
        b_qkv=_columns(g["attn_b_qkv_2"][0, :1280]), b_o=_columns(g["attn_b_o_2"]),
        cw0=_columns(g["ffn_conv_w_2"][:, 0]), cw1=_columns(g["ffn_conv_w_2"][:, 1]),
        cw2=_columns(g["ffn_conv_w_2"][:, 2]), cb=_columns(g["ffn_conv_b_2"]),
        ln_g=_columns(g["sgu_ln_g_2"]), ln_b=_columns(g["sgu_ln_b_2"]),
        cond=np.concatenate([_columns(g["c"]), _columns(g["c_ctx"])], 1),
        b_v=_every(g["attn_b_qkv_2"][0, 1280:]), sinks=_every(g["attn_sinks_2"].reshape(KV_HEADS, 4)[:, SWA_ORDER]), lam=_every(g["lam_a"]))
    arrays = dict(_constants())
    arrays["params"] = np.concatenate([params[k] for k in PARAMS], 1)
    arrays["xT"] = g["x"][0].T.reshape(KT, P, TX).transpose(1, 0, 2)
    arrays["ctxT"] = g["ctx"][0].T.reshape(KT, P, TC).transpose(1, 0, 2)
    arrays["wsT"] = g["sgu_w_s_2"][0].transpose(2, 0, 1)
    arrays["bs"] = _every(g["sgu_b_s_2"]).reshape(P, SG_GROUPS, P)
    pad = np.zeros((8, 16, 127), g["rpb_c"].dtype)
    pad[:, 1:, 48:79] = g["rpb_c"][0]
    toep = np.stack([pad[:, :, 63 - c:127 - c] for c in range(64)], 1)
    arrays["rpb"] = np.concatenate([toep[:, :, 1:16], toep[:, :, 0:15]], 1).reshape(8, P, 15, 64)

    w = g["w_in_even"][0]
    part = [w[:, i * 512:(i + 1) * 512] for i in range(8)]
    arrays["mod0"], arrays["mod1"] = _panels(g["w_mod"][0]), _panels(g["w_mod"][1])
    arrays["even"] = np.concatenate([_panels(w[:, 0:2048]), _alternate(_interleaved(part[5], part[6]),
                                                                       _interleaved(part[4], part[7]))])
    arrays["out0"], arrays["out1"] = _panels(g["w_out"][0]), _panels(g["w_out"][1])
    arrays["odd"] = _panels(g["w_in_odd"][0])
    arrays["qkv"] = _panels(g["attn_w_qkv_2"][0])
    arrays["wo"] = _panels(g["attn_w_o_2"][0])
    for i in range(2):
        arrays[f"ffn{i}_in"] = _interleaved(g["ffn_w_in_2"][i][:, :FF], g["ffn_w_in_2"][i][:, FF:])
        arrays[f"ffn{i}_out"] = _half_panels(g["ffn_w_out_2"][i])
    arrays["sgu_v"] = _panels(g["sgu_w_in_2"][0][:, SG:])
    arrays["sgu_u"] = _panels(g["sgu_w_in_2"][0][:, :SG])
    arrays["sgu_out"] = _half_panels(g["sgu_w_out_2"][0])
    arrays = {k: np.ascontiguousarray(v) for k, v in arrays.items()}

    nc = bacc.Bacc("TRN2", target_bir_lowering=False, num_devices=1, dynamic_dma_scratch_size=1024)
    dram = {k: nc.dram_tensor(f"in_{k}", v.shape, mybir.dt.from_np(v.dtype), kind="ExternalInput").ap()
            for k, v in arrays.items()}
    out = nc.dram_tensor("out", (P, KT, TX), F32, kind="ExternalOutput").ap()
    build_kernel(nc, dram, out)
    result = run_bass_kernel_spmd(nc, [{f"in_{k}": v for k, v in arrays.items()}], core_ids=[0]).results[0]["out"]
    return result.transpose(1, 0, 2).reshape(D, TX).T.reshape(1, TX, D)
```
